# Optimizing a Trainium2 kernel written in Bass

```python
import jax, jax.numpy as jnp
from jax import lax
import numpy as np

D_MODEL = 1024
BATCH = 1
SEQ = 512
DEPTH = 2

N_MIXERS = 2
HEAD_DIM = 64
N_Q_HEADS = D_MODEL // HEAD_DIM
N_KV_HEADS = N_Q_HEADS // 4
GROUP = N_Q_HEADS // N_KV_HEADS
ROT_DIM = HEAD_DIM // 4
ROPE_THETA = 500000.0
WINDOW = 128
BLOCK = 128
IDX_HEADS = 8
IDX_DIM = 64
IDX_ROT_DIM = IDX_DIM // 4
TOPK_MAX = 256
D_FF = 4 * D_MODEL
EPS = 1e-6
N_A = (DEPTH + 1) // 2
N_B = DEPTH // 2
QD = N_Q_HEADS * HEAD_DIM
KVD = N_KV_HEADS * HEAD_DIM
A_IN = QD + 2 * KVD
B_SPLITS = [QD, QD + KVD, QD + 2 * KVD, QD + 2 * KVD + IDX_HEADS * IDX_DIM,
            QD + 2 * KVD + IDX_HEADS * IDX_DIM + IDX_DIM]
B_IN = B_SPLITS[-1] + IDX_HEADS

kernel_name = "hybrid_swa_sink_dsa_trunk"

def rmsnorm(x, g):
    xf = x.astype(jnp.float32)
    y = xf * lax.rsqrt(jnp.mean(xf * xf, axis=-1, keepdims=True) + EPS)
    return (y * g.astype(jnp.float32)).astype(x.dtype)

def partial_rope(x, pos, rot_dim):
    inv = ROPE_THETA ** (-jnp.arange(0, rot_dim, 2, dtype=jnp.float32) / rot_dim)
    ang = pos.astype(jnp.float32)[..., None] * inv
    cos = jnp.cos(ang)[:, :, None, :]
    sin = jnp.sin(ang)[:, :, None, :]
    half = rot_dim // 2
    x1 = x[..., :half].astype(jnp.float32)
    x2 = x[..., half:rot_dim].astype(jnp.float32)
    rot = jnp.concatenate([x1 * cos - x2 * sin, x2 * cos + x1 * sin], axis=-1)
    return jnp.concatenate([rot.astype(x.dtype), x[..., rot_dim:]], axis=-1)

def sliding_window_sink_attention(h, pos, w_in, w_out, sinks):
    B, S, _ = h.shape
    nb = S // BLOCK
    proj = h @ w_in
    q, k, v = jnp.split(proj, [QD, QD + KVD], axis=-1)
    q = partial_rope(q.reshape(B, S, N_Q_HEADS, HEAD_DIM), pos, ROT_DIM)
    k = partial_rope(k.reshape(B, S, N_KV_HEADS, HEAD_DIM), pos, ROT_DIM)
    qb = q.reshape(B, nb, BLOCK, N_KV_HEADS, GROUP, HEAD_DIM)
    kb = k.reshape(B, nb, BLOCK, N_KV_HEADS, HEAD_DIM)
    vb = v.reshape(B, nb, BLOCK, N_KV_HEADS, HEAD_DIM)

    def with_prev(t):
        prev = jnp.concatenate([jnp.zeros_like(t[:, :1]), t[:, :-1]], axis=1)
        return jnp.concatenate([prev, t], axis=2)

    kk, vv = with_prev(kb), with_prev(vb)
    scores = jnp.einsum('bnqhgd,bnkhd->bnhgqk', qb, kk).astype(jnp.float32) * (HEAD_DIM ** -0.5)
    r = jnp.arange(BLOCK)[:, None] + BLOCK
    c = jnp.arange(2 * BLOCK)[None, :]
    diff = r - c
    within = (diff >= 0) & (diff < WINDOW)
    blk = jnp.arange(nb)[:, None, None]
    valid = within[None] & ((blk > 0) | (c[None] >= BLOCK))
    scores = jnp.where(valid[None, :, None, None], scores, -jnp.inf)
    sink = sinks.astype(jnp.float32).reshape(1, 1, N_KV_HEADS, GROUP, 1, 1)
    m = jnp.maximum(jnp.max(scores, axis=-1, keepdims=True), sink)
    p = jnp.exp(scores - m)
    probs = p / (jnp.sum(p, axis=-1, keepdims=True) + jnp.exp(sink - m))
    out = jnp.einsum('bnhgqk,bnkhd->bnqhgd', probs.astype(vv.dtype), vv)
    return out.reshape(B, S, QD) @ w_out

def dsa_sparse_attention(h, pos, w_in, w_out):
    B, S, _ = h.shape
    nb = S // BLOCK
    n_sel = min(TOPK_MAX, S // 4)
    proj = h @ w_in
    q, k, v, qi, ki, wi = jnp.split(proj, B_SPLITS, axis=-1)
    q = partial_rope(q.reshape(B, S, N_Q_HEADS, HEAD_DIM), pos, ROT_DIM)
    k = partial_rope(k.reshape(B, S, N_KV_HEADS, HEAD_DIM), pos, ROT_DIM)
    v = v.reshape(B, S, N_KV_HEADS, HEAD_DIM)
    qi = partial_rope(qi.reshape(B, S, IDX_HEADS, IDX_DIM), pos, IDX_ROT_DIM)
    ki = partial_rope(ki.reshape(B, S, 1, IDX_DIM), pos, IDX_ROT_DIM)[:, :, 0]
    wi = wi * ((IDX_HEADS ** -0.5) * (IDX_DIM ** -0.5))

    qb = jnp.moveaxis(q.reshape(B, nb, BLOCK, N_KV_HEADS, GROUP, HEAD_DIM), 1, 0)
    qib = jnp.moveaxis(qi.reshape(B, nb, BLOCK, IDX_HEADS, IDX_DIM), 1, 0)
    wib = jnp.moveaxis(wi.reshape(B, nb, BLOCK, IDX_HEADS), 1, 0)
    key_pos = jnp.arange(S)

    def block(args):
        q_blk, qi_blk, wi_blk, i = args
        t = i * BLOCK + jnp.arange(BLOCK)
        logits = jnp.einsum('bthd,bsd->bths', qi_blk, ki).astype(jnp.float32)
        score = jnp.einsum('bths,bth->bts', jax.nn.relu(logits), wi_blk.astype(jnp.float32))
        score = jnp.where(key_pos[None, None, :] <= t[None, :, None], score, -jnp.inf)
        _, idx = lax.top_k(score, n_sel)
        sel_ok = idx <= t[None, :, None]
        k_sel = jax.vmap(lambda kb_, ib_: kb_[ib_])(k, idx)
        v_sel = jax.vmap(lambda vb_, ib_: vb_[ib_])(v, idx)
        s = jnp.einsum('bthgd,btkhd->bhgtk', q_blk, k_sel).astype(jnp.float32) * (HEAD_DIM ** -0.5)
        s = jnp.where(sel_ok[:, None, None], s, -jnp.inf)
        pr = jax.nn.softmax(s, axis=-1)
        return jnp.einsum('bhgtk,btkhd->bthgd', pr.astype(v_sel.dtype), v_sel)

    outs = lax.map(block, (qb, qib, wib, jnp.arange(nb)))
    out = jnp.moveaxis(outs, 0, 1).reshape(B, S, QD)
    return out @ w_out

def squared_relu_mlp(h, w_up, w_down):
    a = jax.nn.relu(h @ w_up)
    return (a * a) @ w_down

def setup_inputs(seed: int = 0) -> dict:
    key = jax.random.key(seed)
    ks = jax.random.split(key, 10)
    f32 = jnp.float32
    x = jax.random.normal(ks[0], (BATCH, SEQ, D_MODEL), f32)
    positions = jnp.broadcast_to(jnp.arange(SEQ, dtype=jnp.int32)[None, :], (BATCH, SEQ))
    norm_gains = 1.0 + 0.05 * jax.random.normal(ks[1], (DEPTH, 4, D_MODEL), f32)
    w_mlp_up = jax.random.normal(ks[2], (DEPTH, D_MODEL, D_FF), f32) * D_MODEL ** -0.5
    w_mlp_down = jax.random.normal(ks[3], (DEPTH, D_FF, D_MODEL), f32) * D_FF ** -0.5
    a_w_in = jax.random.normal(ks[4], (N_A, D_MODEL, A_IN), f32) * D_MODEL ** -0.5
    a_w_out = jax.random.normal(ks[5], (N_A, QD, D_MODEL), f32) * QD ** -0.5
    a_sinks = 0.5 * jax.random.normal(ks[6], (N_A, N_Q_HEADS), f32)
    b_w_in = jax.random.normal(ks[7], (N_B, D_MODEL, B_IN), f32) * D_MODEL ** -0.5
    b_w_out = jax.random.normal(ks[8], (N_B, QD, D_MODEL), f32) * QD ** -0.5
    return {"x": x, "positions": positions, "norm_gains": norm_gains,
            "w_mlp_up": w_mlp_up, "w_mlp_down": w_mlp_down,
            "a_w_in": a_w_in, "a_w_out": a_w_out, "a_sinks": a_sinks,
            "b_w_in": b_w_in, "b_w_out": b_w_out}

def reference(x, positions, norm_gains, w_mlp_up, w_mlp_down, a_w_in, a_w_out, a_sinks, b_w_in, b_w_out):
    ia = 0
    ib = 0
    for layer in range(DEPTH):
        g = norm_gains[layer]
        hn = rmsnorm(x, g[0])
        if layer % N_MIXERS == 0:
            mix = sliding_window_sink_attention(hn, positions, a_w_in[ia], a_w_out[ia], a_sinks[ia])
            ia += 1
        else:
            mix = dsa_sparse_attention(hn, positions, b_w_in[ib], b_w_out[ib])
            ib += 1
        x = x + rmsnorm(mix, g[1])
        hn = rmsnorm(x, g[2])
        x = x + rmsnorm(squared_relu_mlp(hn, w_mlp_up[layer], w_mlp_down[layer]), g[3])
    return x


_drawn_inputs = setup_inputs


def setup_inputs(seed=0):
    import zlib

    import numpy as np

    out = dict(_drawn_inputs(seed))
    spreads = {}
    factors = {'a_sinks': 2.935}
    for name, (base, spread) in spreads.items():
        noise = np.random.default_rng([zlib.crc32(name.encode()), seed]).standard_normal(out[name].shape)
        drawn = base * np.exp(spread * noise) if base else spread * noise
        out[name] = __import__('jax').numpy.asarray(drawn.astype(out[name].dtype))
    for name, factor in factors.items():
        out[name] = (out[name] * factor).astype(out[name].dtype)
    return out
```

```python
import concourse.bass as bass
from concourse import mybir
from contextlib import ExitStack

P = 128
D, SEQ, DEPTH = 1024, 512, 2
NH, NKV, HD = 16, 4, 64
GROUP = NH // NKV
FF = 4 * D
IDX_HEADS, IDX_DIM = 8, 64
TOPK = min(256, SEQ // 4)
EPS = 1e-6
KT = D // P
NB = SEQ // P
QD, KVD = NH * HD, NKV * HD
SCALE = HD ** -0.5
IDX_SCALE = IDX_HEADS ** -0.5 * IDX_DIM ** -0.5
ROT_DIM = HD // 4
NEG = -1.0e30
TAKEN = -3.0e38

UNIT = 4 * 512
QUARTERS = 4
HID = FF // QUARTERS // P
MLP_UNITS, MLP_TILES, MLP_GROUPS = 8, 16, 4
A_IN_GROUPS, OUT_GROUPS = 3, 2
IDX_COLS = 88
WI_AT = 80

PI = 3.141592653589793
TWO_PI_PARTS = (6.25, 0.033203125, 2 * PI - 6.25 - 0.033203125)
ROUND = 12582912.0
PI_IN = 3.1415925
TRIG_OPS, SETUP_OPS = 8, 6


def counts():
    at, u, t, g = {}, 0, 0, 0
    for name, du, dt, dg in (
        ("in0", 6, 12, 3), ("out0", 4, 8, 2), ("mlp0", 32, 64, 16),
        ("qi", 2, 4, 1), ("ki", 1, 1, 0), ("in1", 6, 12, 3), ("out1", 4, 8, 2), ("mlp1", 32, 64, 16),
        ("end", 0, 0, 0),
    ):
        at[name] = (u, t, g)
        u, t, g = u + du, t + dt, g + dg
    return at


AT = counts()


def key_blocks(layer, i):
    return list(range(i + 1)) if layer else list(range(max(0, i - 1), i + 1))


PT_PLACES = 4

STEPS = [(layer, i, g) for layer in range(2) for i in range(NB) for g in range(NKV)]
PT_AT = [0]
for _l, _i, _g in STEPS:
    PT_AT.append(PT_AT[-1] + len(key_blocks(_l, _i)))


def blocks_of(base, j, first, end):
    if not 0 <= j < 16:
        return []
    return list(range(PT_AT[base + j], PT_AT[base + j + 1]))[first:end]


def rb_bank(norm):
    before_unit = ("in0", "mlp0", "mlp0", "qi", "qi", "mlp1", "mlp1", "end")[norm]
    return (AT[before_unit][1] + (6 if norm in (0, 2, 4, 6) else 4)) % 8


def ssq_bank(norm):
    return (rb_bank(norm) + 1) % 8


def idx_bank(X):
    return (AT["in1"][1] + 4 + X % 4) % 8


def x_bank(k):
    return 4 + k % 4


def hybrid_trunk(nc, x, positions, gains, w_up, w_down, a_in, a_out, sinks, b_in, b_out, consts, out):
    f32, f32r, i32 = mybir.dt.float32, mybir.dt.float32r, mybir.dt.int32
    ALU, ACT = mybir.AluOpType, mybir.ActivationFunctionType

    ctx = ExitStack()
    with ctx:
        def sb(name, shape, dt=f32):
            return ctx.enter_context(nc.sbuf_tensor(name, shape, dt))

        def sem(name):
            return ctx.enter_context(nc.semaphore(name))

        xT = sb("xT", [P, KT, SEQ])
        in_hi, in_lo = sb("in_hi", [P, KT, SEQ], f32r), sb("in_lo", [P, KT, SEQ], f32r)
        act_hi, act_lo = sb("act_hi", [P, KT, SEQ], f32r), sb("act_lo", [P, KT, SEQ], f32r)
        w_raw = sb("w_raw", [P, 2, UNIT])
        w_hi, w_lo = sb("w_hi", [P, 2, UNIT], f32r), sb("w_lo", [P, 2, UNIT], f32r)
        k_hi, k_lo = sb("k_hi", [P, 2, SEQ], f32r), sb("k_lo", [P, 2, SEQ], f32r)
        v_hi, v_lo = sb("v_hi", [P, NB, 9 * HD], f32r), sb("v_lo", [P, NB, 9 * HD], f32r)
        cos, sin = sb("cos", [P, SEQ]), sb("sin", [P, SEQ])
        cos_r, sin_r = sb("cos_r", [P, SEQ]), sb("sin_r", [P, SEQ])
        rb = sb("rb", [P, SEQ])
        work = sb("work", [P, 7168])
        pt_hi, pt_lo = sb("pt_hi", [P, PT_PLACES, SEQ], f32r), sb("pt_lo", [P, PT_PLACES, SEQ], f32r)
        score = sb("score", [P, NB - 1, SEQ])
        const = sb("const", [P, 2 * P + 1])
        gT = sb("gT", [P, DEPTH * 4 * KT])
        g_rows = sb("g_rows", [DEPTH * 4 * KT, P])
        band = sb("band", [P, 2 * P])
        ones = sb("ones", [P, P])
        diag = sb("diag", [P, NB, P])
        small = sb("small", [P, 128])
        pos_i = sb("pos_i", [P, SEQ], i32)
        banks = [ctx.enter_context(nc.psum_tensor(f"bank{i}", [P, 512], f32)) for i in range(8)]

        ident, rot_t, inv_freq = const[:, 0:P], const[:, P:2 * P], const[:, 2 * P:2 * P + 1]
        own = band[:, P:2 * P]
        x_rows = work[:, 0:NB * D].rearrange("p (j n) -> p j n", j=NB)
        y = work[:, 0:KT * SEQ].rearrange("p (k n) -> p k n", k=KT)
        tmp_a = work[:, 4096:5120].rearrange("p (k n) -> p k n", k=2)
        tmp_b = work[:, 5120:6656].rearrange("p (k n) -> p k n", k=3)
        raw = work[:, 0:2048].rearrange("p (k n) -> p k n", k=4)
        roped = work[:, 2048:4096].rearrange("p (k n) -> p k n", k=4)
        turned = work[:, 4096:5120].rearrange("p (k n) -> p k n", k=2)
        relu = work[:, 5120:6144].rearrange("p (k n) -> p k n", k=2)
        probs = work[:, 0:6144].rearrange("p (s r n) -> p s r n", s=3, r=GROUP)
        out_rows = work[:, 0:NB * D].rearrange("p (j n) -> p j n", j=NB)
        sq = score[:, 0:2, :]
        sq_sum = score[:, 2, :]
        ang, turns, cos_arg = work[:, 4096:4608], work[:, 4608:5120], work[:, 5120:5632]
        ms, rstd, half_neg = small[:, 0:4], small[:, 4:8], small[:, 8:12]
        half_pi = small[:, 12:13]
        ceiling = small[:, 13:14]
        sink = small[:, 16:32]
        neg_sink = small[:, 92:108]
        neg_max = small[:, 44:56].rearrange("p (s r) -> p s r", s=3)
        row_sum = small[:, 56:68].rearrange("p (s r) -> p s r", s=3)
        inv_sum = small[:, 68:80].rearrange("p (s r) -> p s r", s=3)
        sink_e = small[:, 80:92].rearrange("p (s r) -> p s r", s=3)
        top8 = sb("top8", [P, NB - 1, 8])
        wi = sb("wi", [P, NB, IDX_HEADS])

        x_in, const_in, small_in = sem("x_in"), sem("const_in"), sem("small_in")
        w_in = [sem("w_in0"), sem("w_in1")]
        w_hi_done, w_lo_done = sem("w_hi_done"), sem("w_lo_done")
        half_used = sem("half_used")
        tile_done, tile_out = sem("tile_done"), sem("tile_out")
        gains_t, gains_out = sem("gains_t"), sem("gains_out")
        x_t, x_ready = sem("x_t"), sem("x_ready")
        in_hi_done, in_lo_done = sem("in_hi_done"), sem("in_lo_done")
        sq_done, sq_added, sq_zero = sem("sq_done"), sem("sq_added"), sem("sq_zero")
        ssq_done, ms_done, rstd_done = sem("ssq_done"), sem("ms_done"), sem("rstd_done")
        diag_done, rb_done, rb_out = sem("diag_done"), sem("rb_done"), sem("rb_out")
        setup_v, setup_g, trig, trig_v = sem("setup_v"), sem("setup_g"), sem("trig"), sem("trig_v")
        cs_done = sem("cs_done")
        raw_out, rot_done, rope_v, rope_done = sem("raw_out"), sem("rot_done"), sem("rope_v"), sem("rope_done")
        rope_hi, rope_lo = sem("rope_hi"), sem("rope_lo")
        v_scaled = sem("v_scaled")
        vt_done, v_hi_done, v_lo_done = sem("vt_done"), sem("v_hi_done"), sem("v_lo_done")
        ki_dup, wi_t, wi_out = sem("ki_dup"), sem("wi_t"), sem("wi_out")
        idx_ready, idx_relu, idx_acc, top_v = sem("idx_ready"), sem("idx_relu"), sem("idx_acc"), sem("top_v")
        s_ready, s_masked, exp_done, p_last_done = sem("s_ready"), sem("s_masked"), sem("exp_done"), sem("p_last_done")
        sink_d, sink_x, sum_v, inv_done, p_done = (sem("sink_d"), sem("sink_x"), sem("sum_v"),
                                                    sem("inv_done"), sem("p_done"))
        pt_ready, pt_hi_done, pt_lo_done, pv_done = (sem("pt_ready"), sem("pt_hi_done"),
                                                     sem("pt_lo_done"), sem("pv_done"))
        o_hi_done, o_lo_done = sem("o_hi_done"), sem("o_lo_done")
        y_zero, upd = sem("y_zero"), sem("upd")
        relu2, act_hi_done, act_lo_done = sem("relu2"), sem("act_hi_done"), sem("act_lo_done")
        out_t, out_v, out_in = sem("out_t"), sem("out_v"), sem("out_in")

        block = ctx.enter_context(nc.Block())

        ROPE_AT = {"in0": 0, "qi": 10, "ki": 14, "in1": 15}
        V_AT = {"in0": 0, "in1": 2}
        PRE = {"in0": 0, "mlp0": 1, "qi": 2, "mlp1": 3}
        NORM = {"in0": 0, "post0": 1, "mlp0": 2, "mlp_post0": 3, "qi": 4, "post1": 5, "mlp1": 6, "mlp_post1": 7}

        def rope_place(name, m):
            if name == "ki":
                return pt_hi[:, 0, :], pt_lo[:, 0, :]
            if m >= KT:
                return k_hi[:, m - KT, :], k_lo[:, m - KT, :]
            return act_hi[:, m, :], act_lo[:, m, :]

        def v_place(v, m):
            return v[:, :, HD + 256 * m:HD + 256 * m + 256].rearrange("p j (a c) -> p j a c", c=P)[:, :, :, 0:HD]

        def o_place(t, N):
            _, i, g = STEPS[N]
            p = g // 2
            return t[:, 4 * p:4 * p + 4, i * P:(i + 1) * P]

        def mlp_used(it, j, t0, g0):
            if j % 2 == 0:
                return half_used, it * MLP_GROUPS + (g0 + j // 2 + 1)
            return tile_done, it * MLP_TILES + (t0 + 4 * (j // 2) + 4)

        def gain(layer, n, k):
            c = (layer * 4 + n) * KT + k
            return gT[:, c:c + 1]

        @block.sync
        def _(sp):
            def load(u, src, it=0, d_it=0):
                slot = u % 2
                dst = w_raw[:, slot, :].rearrange("p (k n) -> p k n", k=4)
                if u >= 2:
                    sp.wait_ge(w_lo_done, it * d_it + (u - 1))
                for a in range(2):
                    sp.dma_start(dst[64 * a:64 * a + 64], src(a)).then_inc(w_in[slot], 16)

            def plain(w, row, col):
                v = w[row:row + 512, col:col + 512].rearrange("(k p) n -> p k n", p=P)
                return lambda a: v[64 * a:64 * a + 64]

            for j in range(NB):
                sp.dma_start(x_rows[:, j, :], x[j * P:(j + 1) * P, :]).then_inc(x_in, 16)

            def load_out(name, w):
                u0 = AT[name][0]
                for c in range(OUT_GROUPS):
                    for p in range(2):
                        def src(a):
                            r0 = 512 * p + 256 * a
                            return w[r0:r0 + 256, 512 * c:512 * c + 512].rearrange("(r c) n -> c r n", c=HD)
                        load(u0 + 2 * c + p, src)

            def load_mlp(layer):
                u0 = AT[f"mlp{layer}"][0]

                def quarter(q, it):
                    for j in range(MLP_UNITS):
                        g, h = (j % 4) // 2, j % 2
                        if j < 4:
                            rows, cols = slice(512 * h, 512 * h + 512), bass.ds(q * 1024 + 512 * g, 512)
                            w = w_up[layer]
                        else:
                            rows, cols = bass.ds(q * 1024 + 512 * h, 512), slice(512 * g, 512 * g + 512)
                            w = w_down[layer]
                        v = w[rows, cols].rearrange("(k p) n -> p k n", p=P)
                        load(u0 + j, lambda a: v[64 * a:64 * a + 64], it, MLP_UNITS)
                with sp.Fori(0, QUARTERS) as q:
                    quarter(q, q)

            for g in range(A_IN_GROUPS):
                for h in range(2):
                    load(2 * g + h, plain(a_in, 512 * h, 512 * g))
            load_out("out0", a_out)
            load_mlp(0)
            for h in range(2):
                load(AT["qi"][0] + h, plain(b_in, 512 * h, QD + 2 * KVD))
            u = AT["ki"][0]
            dst = w_raw[:, u % 2, 0:KT * IDX_COLS].rearrange("p (k n) -> p k n", k=KT)
            c0 = QD + 2 * KVD + IDX_HEADS * IDX_DIM
            sp.wait_ge(w_lo_done, u - 1)
            sp.dma_start(dst[:, :, 0:IDX_DIM], b_in[:, c0:c0 + IDX_DIM].rearrange("(k p) n -> p k n", p=P)).then_inc(w_in[u % 2], 16)
            sp.dma_start(dst[:, :, WI_AT:WI_AT + IDX_HEADS],
                         b_in[:, c0 + IDX_DIM:c0 + IDX_DIM + IDX_HEADS].rearrange("(k p) n -> p k n", p=P)).then_inc(w_in[u % 2], 16)
            for g in range(A_IN_GROUPS):
                for h in range(2):
                    load(AT["in1"][0] + 2 * g + h, plain(b_in, 512 * h, 512 * g))
            load_out("out1", b_out)
            load_mlp(1)
            for half in range(2):
                for j in range(NB):
                    sp.wait_ge(out_v, half * NB + j + 1)
                    sp.dma_start(out[j * P:(j + 1) * P, half * 512:half * 512 + 512],
                                 out_rows[:, j, half * 512:half * 512 + 512]).then_inc(out_in, 16)
            sp.wait_ge(out_in, 16 * 2 * NB)

        @block.gpsimd
        def _(pool):
            nc.gpsimd.memset(band[:], 0.0).then_inc(setup_g, 1)
            nc.gpsimd.memset(ones[:], 1.0).then_inc(setup_g, 1)
            pool.wait_ge(setup_g, 1)
            nc.gpsimd.affine_select(out=band[:, 0:P], in_=band[:, 0:P], compare_op=ALU.is_gt, fill=NEG, base=0,
                                    pattern=[[1, P]], channel_multiplier=-1).then_inc(setup_g, 1)
            nc.gpsimd.affine_select(out=band[:, P:2 * P], in_=band[:, P:2 * P], compare_op=ALU.is_ge, fill=NEG, base=0,
                                    pattern=[[-1, P]], channel_multiplier=1).then_inc(setup_g, 1)

            def norm_sums(n):
                if n:
                    pool.wait_ge(ssq_done, n)
                if n == NORM["post1"]:
                    pool.wait_ge(p_done, 3 * len(STEPS))
                nc.gpsimd.memset(sq_sum, 0.0).then_inc(sq_zero, 1)
                pool.wait_ge(sq_zero, n + 1)
                for k in range(KT - 1):
                    pool.wait_ge(sq_done, n * KT + k + 1)
                    if k:
                        pool.wait_ge(sq_added, n * (KT - 1) + k)
                    nc.gpsimd.tensor_tensor(sq_sum, sq_sum, sq[:, k % 2, :], ALU.add).then_inc(sq_added, 1)
                pool.wait_ge(ms_done, n + 1)
                nc.gpsimd.tensor_tensor(rstd, ms, half_neg, ALU.pow).then_inc(rstd_done, 1)

            pool.wait_ge(setup_v, 1)
            for layer in range(DEPTH):
                norm_sums(NORM[("in0", "qi")[layer]])
                norm_sums(NORM[f"post{layer}"])
                norm_sums(NORM[f"mlp{layer}"])
                pool.wait_ge(upd, (2 * layer + 1) * KT)
                nc.gpsimd.memset(y, 0.0).then_inc(y_zero, 1)
                norm_sums(NORM[f"mlp_post{layer}"])

        @block.scalar
        def _(act):
            act.dma_start(const[:], consts).then_inc(const_in, 16)
            act.dma_start(g_rows[:], gains).then_inc(const_in, 16)
            act.dma_start(sink, sinks.broadcast_to([P, NH])).then_inc(small_in, 16)
            act.dma_start(pos_i[:], positions.broadcast_to([P, SEQ])).then_inc(small_in, 16)

            def unit_free(u, done):
                if done is not None:
                    act.wait_ge(*done)

            def split(u, done, heads=False, cols=UNIT, it=0, d_it=0):
                slot = u % 2
                act.wait_ge(w_in[slot], it * (16 * d_it) + 32 * (u // 2 + 1))
                unit_free(u, done)
                if heads:
                    s = w_raw[:, slot, :].rearrange("p (k a r c) -> p k a r c", k=4, a=2, r=4)
                    d = w_hi[:, slot, :].rearrange("p (k r a c) -> p k r a c", k=4, a=2, r=4)
                    for a in range(2):
                        last = nc.scalar.activation(d[:, :, :, a, :], s[:, :, a, :, :], ACT.Copy)
                else:
                    last = nc.scalar.activation(w_hi[:, slot, 0:cols], w_raw[:, slot, 0:cols], ACT.Copy)
                last.then_inc(w_hi_done, 1)

            def feed(n, pre, layer, which, k):
                act.wait_ge(x_ready, n * KT + k + 1)
                nc.scalar.activation(in_hi[:, k, :], xT[:, k, :], ACT.Copy, scale=gain(layer, which, k)).then_inc(in_hi_done, 1)

            def square(norm, src, k):
                if k >= 2:
                    act.wait_ge(sq_added, norm * (KT - 1) + k - 1)
                elif norm:
                    act.wait_ge(ssq_done, norm)
                nc.scalar.activation(sq[:, k % 2, :], src, ACT.Square).then_inc(sq_done, 1)

            def rb_copy(pre, norm):
                act.wait_ge(rb_done, norm + 1)
                nc.scalar.activation(rb[:], banks[rb_bank(norm)][:], ACT.Copy).then_inc(rb_out, 1)

            def copy_raw(name, m):
                T, R = AT[name][1] + m, ROPE_AT[name] + m
                act.wait_ge(tile_done, T + 1)
                if R >= 4:
                    act.wait_ge(rope_done, R - 3)
                rows = IDX_COLS if name == "ki" else P
                nc.scalar.activation(raw[0:rows, R % 4, :], banks[T % 8][0:rows, :], ACT.Copy).then_inc(raw_out, 1)

            def hi_rope(name, m):
                R = ROPE_AT[name] + m
                act.wait_ge(rope_done, R + 1)
                rows = IDX_DIM if name == "ki" else P
                nc.scalar.activation(rope_place(name, m)[0][0:rows], roped[0:rows, R % 4, :], ACT.Copy).then_inc(rope_hi, 1)

            def hi_v(name, m):
                V = V_AT[name] + m
                act.wait_ge(vt_done, V + 1)
                bank = banks[(AT[name][1] + 10 + m) % 8]
                nc.scalar.activation(v_place(v_hi, m), bank[:].rearrange("p (j a c) -> p j a c", j=NB, a=2),
                                     ACT.Copy).then_inc(v_hi_done, 1)

            def expo(N, r):
                layer, i, g = STEPS[N]
                s, W = N % 3, len(key_blocks(layer, i)) * P
                act.wait_ge(s_masked, 4 * N + r + 1)
                nc.scalar.activation(probs[:, s, r, 0:W], probs[:, s, r, 0:W], ACT.Exp,
                                     bias=neg_max[:, s, r:r + 1], scale=-1.0,
                                     accum_out=row_sum[:, s, r:r + 1]).then_inc(exp_done, 1)
                if layer == 0 and r == GROUP - 1:
                    act.wait_ge(sink_d, N + 1)
                    nc.scalar.activation(sink_e[:, s, :], sink_e[:, s, :], ACT.Exp).then_inc(sink_x, 1)

            def normed_last(N):
                layer, i, g = STEPS[N]
                s, W = N % 3, len(key_blocks(layer, i)) * P
                act.wait_ge(inv_done, N + 1)
                nc.scalar.activation(probs[:, s, GROUP - 1, 0:W], probs[:, s, GROUP - 1, 0:W], ACT.Copy,
                                     scale=inv_sum[:, s, GROUP - 1:GROUP]).then_inc(p_last_done, 1)

            def pt_high(K):
                act.wait_ge(pt_ready, K + 1)
                if K >= PT_PLACES:
                    act.wait_ge(pv_done, K - PT_PLACES + 1)
                nc.scalar.activation(pt_hi[:, K % PT_PLACES, :], banks[4 + K % 2][:], ACT.Copy).then_inc(pt_hi_done, 1)

            def o_high(N):
                act.wait_ge(pv_done, PT_AT[N + 1])
                nc.scalar.activation(o_place(in_hi, N), banks[6 + (N // 2) % 2][:].rearrange("p (r n) -> p r n", r=GROUP),
                                     ACT.Copy).then_inc(o_hi_done, 1)

            def attention(layer):
                base = 16 * layer
                for j in range(19):
                    N = base + j
                    for K in blocks_of(base, j - 2, 2, 4):
                        pt_high(K)
                    if j >= 4 and j % 2 == 0:
                        o_high(N - 3)
                    if j < 16:
                        expo(N, 0)
                        expo(N, 1)
                    if 1 <= j < 17:
                        normed_last(N - 1)
                    for c in range(2):
                        for K in blocks_of(base, j - 1, c, c + 1):
                            pt_high(K)
                        if j < 16:
                            expo(N, 2 + c)

            def mlp(layer):
                u0, t0, g0 = AT[f"mlp{layer}"]

                def quarter(it, last):
                    def sp(j):
                        split(u0 + j, mlp_used(it, j - 2, t0, g0), it=it, d_it=MLP_UNITS)

                    def hid(fs):
                        for f in fs:
                            act.wait_ge(relu2, it * HID + (layer * QUARTERS * HID + f + 1))
                            nc.scalar.activation(act_hi[:, f, :], tmp_b[:, f % 3, :], ACT.Copy).then_inc(act_hi_done, 1)
                    sp(2)
                    hid(range(0, 4))
                    sp(3)
                    sp(4)
                    hid(range(4, 8))
                    for j in (5, 6, 7):
                        sp(j)
                    if not (last and layer):
                        sp(8)
                    if not last:
                        sp(9)

                quarter(0, False)
                with act.Fori(1, QUARTERS - 1) as it:
                    quarter(it, False)
                quarter(QUARTERS - 1, True)
                for k in range(KT):
                    act.wait_ge(tile_out, t0 + MLP_TILES * (QUARTERS - 1) + 8 + k + 1)
                    square(NORM[f"mlp_post{layer}"], y[:, k, :], k)

            def feed_all(name, n, layer, which):
                for k in range(KT):
                    feed(n, PRE[name], layer, which, k)
                    square(NORM[name], xT[:, k, :], k)

            split(0, None, heads=True)
            split(1, None, heads=True)
            act.wait_ge(gains_out, 1)
            feed_all("in0", 0, 0, 0)
            act.wait_ge(setup_v, 2)
            act.wait_ge(trig_v, TRIG_OPS)
            nc.scalar.activation(sin[:], ang, ACT.Sin).then_inc(trig, 1)
            nc.scalar.activation(cos_arg, ang, ACT.Abs).then_inc(trig, 1)
            act.wait_ge(trig, 2)
            nc.scalar.activation(cos[:], cos_arg, ACT.Sin, bias=half_pi, scale=-1.0).then_inc(trig, 1)

            for layer in range(DEPTH):
                name = f"in{layer}"
                u0, t0, g0 = AT[name]
                if layer == 0:
                    rb_copy(0, NORM["in0"])
                else:
                    uq, tq, gq = AT["qi"]
                    uk, tk, _ = AT["ki"]
                    feed_all("qi", 2, 1, 0)
                    split(uq + 1, (tile_done, tq))
                    act.wait_ge(setup_v, SETUP_OPS + 1)
                    split(uk, (half_used, gq + 1), cols=KT * IDX_COLS)
                    rb_copy(2, NORM["qi"])
                    for m in range(4):
                        copy_raw("qi", m)
                    split(u0, (tile_done, tq + 4), heads=True)
                    for m in range(4):
                        hi_rope("qi", m)
                    copy_raw("ki", 0)
                    split(u0 + 1, (tile_done, tk + 1), heads=True)
                    hi_rope("ki", 0)
                    act.wait_ge(rope_hi, ROPE_AT["ki"] + 1)
                    act.wait_ge(rope_lo, ROPE_AT["ki"] + 1)
                    act.dma_start(pt_hi[64:128, 0, :].bitcast(f32), pt_hi[0:64, 0, :].bitcast(f32)).then_inc(ki_dup, 16)
                    act.dma_start(pt_lo[64:128, 0, :].bitcast(f32), pt_lo[0:64, 0, :].bitcast(f32)).then_inc(ki_dup, 16)
                for g in range(A_IN_GROUPS):
                    split(u0 + 2 * g + 2, (half_used, g0 + g + 1), heads=g < 1)
                    if g < 2:
                        for m in range(4 * g, 4 * g + 4):
                            copy_raw(name, m)
                    else:
                        for m in (8, 9):
                            copy_raw(name, m)
                    split(u0 + 2 * g + 3, (tile_done, t0 + 4 * g + 4), heads=g < 1)
                    if layer and g == 0:
                        for X in range(8 * (NB - 1)):
                            W = (X // 8 + 2) * P
                            act.wait_ge(idx_ready, X + 1)
                            if X >= 2:
                                act.wait_ge(idx_acc, X - 1)
                            nc.scalar.activation(relu[:, X % 2, 0:W], banks[idx_bank(X)][:, 0:W], ACT.Relu).then_inc(idx_relu, 1)
                    for m in (range(4 * g, 4 * g + 4) if g < 2 else (8, 9)):
                        hi_rope(name, m)
                    if g == 2:
                        for m in range(2):
                            hi_v(name, m)
                attention(layer)
                u0, t0, g0 = AT[f"out{layer}"]
                for g in range(OUT_GROUPS):
                    split(u0 + 2 * g + 2, (half_used, g0 + g + 1))
                    for k in range(4 * g, 4 * g + 4):
                        act.wait_ge(tile_out, t0 + k + 1)
                        square(NORM[f"post{layer}"], y[:, k, :], k)
                    if g == 0:
                        split(u0 + 3, (tile_done, t0 + 4))
                feed_all(f"mlp{layer}", 2 * layer + 1, layer, 2)
                split(u0 + 5, (tile_done, t0 + 8))
                rb_copy(2 * layer + 1, NORM[f"mlp{layer}"])
                mlp(layer)

        @block.vector
        def _(dve):
            def split(u, done, heads=False, cols=UNIT, it=0, d_it=0):
                slot = u % 2
                dve.wait_ge(w_hi_done, it * d_it + (u + 1))
                if heads:
                    s = w_raw[:, slot, :].rearrange("p (k a r c) -> p k a r c", k=4, a=2, r=4)
                    h = w_hi[:, slot, :].bitcast(f32).rearrange("p (k r a c) -> p k r a c", k=4, a=2, r=4)
                    d = w_lo[:, slot, :].rearrange("p (k r a c) -> p k r a c", k=4, a=2, r=4)
                    for a in range(2):
                        last = nc.vector.tensor_tensor(d[:, :, :, a, :], s[:, :, a, :, :], h[:, :, :, a, :], ALU.subtract)
                else:
                    last = nc.vector.tensor_tensor(w_lo[:, slot, 0:cols], w_raw[:, slot, 0:cols],
                                                   w_hi[:, slot, 0:cols].bitcast(f32), ALU.subtract)
                last.then_inc(w_lo_done, 1)

            def feed_lo(n, layer, which, k):
                dve.wait_ge(in_hi_done, n * KT + k + 1)
                nc.vector.scalar_tensor_tensor(out=in_lo[:, k, :], in0=xT[:, k, :], scalar=gain(layer, which, k),
                                               in1=in_hi[:, k, :].bitcast(f32), op0=ALU.mult,
                                               op1=ALU.subtract).then_inc(in_lo_done, 1)

            def stats(norm):
                dve.wait_ge(ssq_done, norm + 1)
                nc.vector.tensor_scalar(ms, banks[ssq_bank(norm)][:, 0:NB], 1.0 / D, EPS, ALU.mult, ALU.add).then_inc(ms_done, 1)
                dve.wait_ge(rstd_done, norm + 1)
                for j in range(NB):
                    nc.vector.tensor_scalar(diag[:, j, :], ident, rstd[:, j:j + 1], None, ALU.mult).then_inc(diag_done, 1)

            def update(norm, n, layer, which, nxt):
                dve.wait_ge(rb_done, norm + 1)
                for k in range(KT + 1):
                    if k < KT:
                        if k >= 2:
                            dve.wait_ge(x_ready, n * KT + k - 1)
                        nc.vector.scalar_tensor_tensor(out=tmp_a[:, k % 2, :], in0=y[:, k, :], scalar=gain(layer, which, k),
                                                       in1=banks[rb_bank(norm)][:], op0=ALU.mult, op1=ALU.mult).then_inc(upd, 1)
                    if k and nxt:
                        feed_lo(n, *nxt, k - 1)
                    if k < KT:
                        dve.wait_ge(upd, (n - 1) * KT + k + 1)
                        nc.vector.tensor_tensor(xT[:, k, :], xT[:, k, :], tmp_a[:, k % 2, :], ALU.add).then_inc(x_ready, 1)

            def scaled_tables(c):
                nc.vector.tensor_tensor(cos_r[:], cos[:], rb[:], ALU.mult).then_inc(cs_done, 1)
                nc.vector.tensor_tensor(sin_r[:], sin[:], rb[:], ALU.mult).then_inc(cs_done, 1)
                dve.wait_ge(cs_done, 2 * c + 2)

            def rope_first(name, m):
                R = ROPE_AT[name] + m
                rows = IDX_COLS if name == "ki" else P
                dve.wait_ge(raw_out, R + 1)
                if R >= 4:
                    dve.wait_ge(rope_lo, R - 3)
                if R == ROPE_AT["ki"] + 4:
                    dve.wait_ge(wi_t, 1)
                nc.vector.tensor_tensor(roped[0:rows, R % 4, :], raw[0:rows, R % 4, :], cos_r[0:rows], ALU.mult).then_inc(rope_v, 1)

            def rope_second(name, m):
                T, R = AT[name][1] + m, ROPE_AT[name] + m
                rows = IDX_COLS if name == "ki" else P
                dve.wait_ge(rot_done, R + 1)
                if R >= 2:
                    dve.wait_ge(rope_done, R - 1)
                nc.vector.tensor_tensor(turned[0:rows, R % 2, :], banks[T % 8][0:rows, :], sin_r[0:rows], ALU.mult).then_inc(tile_out, 1)
                dve.wait_ge(tile_out, T + 1)
                dve.wait_ge(rope_v, R + 1)
                nc.vector.tensor_tensor(roped[0:rows, R % 4, :], roped[0:rows, R % 4, :], turned[0:rows, R % 2, :], ALU.add).then_inc(rope_done, 1)

            def rope_low(name, m):
                R = ROPE_AT[name] + m
                rows = IDX_DIM if name == "ki" else P
                hi, lo = rope_place(name, m)
                dve.wait_ge(rope_hi, R + 1)
                nc.vector.tensor_tensor(lo[0:rows], roped[0:rows, R % 4, :], hi[0:rows].bitcast(f32), ALU.subtract).then_inc(rope_lo, 1)

            def masked(N, r):
                layer, i, g = STEPS[N]
                s, kbs = N % 3, key_blocks(layer, i)
                W = len(kbs) * P
                dve.wait_ge(s_ready, 4 * N + r + 1)
                if r == 0 and N % 16 >= 3:
                    dve.wait_ge(pt_ready, PT_AT[N - 2])
                if i == 0:
                    mask = own
                elif layer == 0:
                    mask = band[:]
                else:
                    mask = score[:, i - 1, 0:W]
                h = 4 * g + r
                nc.vector.tensor_tensor_reduce(out=probs[:, s, r, 0:W], in0=banks[r][:, 0:W], in1=mask, scale=-SCALE,
                                               scalar=neg_sink[:, h:h + 1] if layer == 0 else ceiling,
                                               op0=ALU.add, op1=ALU.min, accum_out=neg_max[:, s, r:r + 1]).then_inc(s_masked, 1)
                if layer == 0 and r == GROUP - 1:
                    dve.wait_ge(s_masked, 4 * N + 4)
                    nc.vector.tensor_tensor(sink_e[:, s, :], sink[:, 4 * g:4 * g + 4], neg_max[:, s, :], ALU.add).then_inc(sink_d, 1)

            def inverse(N):
                layer, i, g = STEPS[N]
                s = N % 3
                dve.wait_ge(exp_done, 4 * N + 4)
                if layer == 0:
                    dve.wait_ge(sink_x, N + 1)
                    nc.vector.tensor_tensor(row_sum[:, s, :], row_sum[:, s, :], sink_e[:, s, :], ALU.add).then_inc(sum_v, 1)
                    dve.wait_ge(sum_v, N + 1)
                nc.vector.reciprocal(inv_sum[:, s, :], row_sum[:, s, :]).then_inc(inv_done, 1)
                dve.wait_ge(inv_done, N + 1)

            def normed(N, r):
                layer, i, g = STEPS[N]
                s, W = N % 3, len(key_blocks(layer, i)) * P
                nc.vector.tensor_scalar(probs[:, s, r, 0:W], probs[:, s, r, 0:W], inv_sum[:, s, r:r + 1], None, ALU.mult).then_inc(p_done, 1)

            def pt_low(K):
                dve.wait_ge(pt_hi_done, K + 1)
                nc.vector.tensor_tensor(pt_lo[:, K % PT_PLACES, :], banks[4 + K % 2][:], pt_hi[:, K % PT_PLACES, :].bitcast(f32),
                                        ALU.subtract).then_inc(pt_lo_done, 1)

            def o_low(N):
                pair = N // 2
                dve.wait_ge(o_hi_done, pair + 1)
                nc.vector.tensor_tensor(o_place(in_lo, N), banks[6 + pair % 2][:].rearrange("p (r n) -> p r n", r=GROUP),
                                        o_place(in_hi, N).bitcast(f32), ALU.subtract).then_inc(o_lo_done, 1)

            def attention(layer, extra):
                base = 16 * layer
                for j in range(19):
                    N = base + j
                    for K in blocks_of(base, j - 2, 0, 2):
                        pt_low(K)
                    for c in range(2):
                        if j < 16:
                            masked(N, c)
                        for K in blocks_of(base, j - 2, 2 + c, 3 + c):
                            pt_low(K)
                    if 1 <= j < 17:
                        inverse(N - 1)
                        for r in range(GROUP - 1):
                            normed(N - 1, r)
                    if j >= 4 and j % 2 == 0:
                        o_low(N - 3)
                    for r in range(2, GROUP):
                        if j < 16:
                            masked(N, r)
                    extra(j)

            top_n = [0]

            def top_wait():
                dve.wait_ge(top_v, top_n[0])

            def top_round(bs):
                for b in bs:
                    nc.vector.max(top8[:, b - 1, :], score[:, b - 1, 0:(b + 1) * P]).then_inc(top_v, 1)
                top_n[0] += len(bs)
                top_wait()
                for b in bs:
                    v = score[:, b - 1, 0:(b + 1) * P]
                    nc.vector.match_replace(v, top8[:, b - 1, :], v, TAKEN).then_inc(top_v, 1)
                top_n[0] += len(bs)
                top_wait()

            def top_mask(bs):
                for b in bs:
                    v = score[:, b - 1, 0:(b + 1) * P]
                    nc.vector.tensor_scalar(v, v, TAKEN / 2, NEG, ALU.is_gt, ALU.mult).then_inc(top_v, 1)
                top_n[0] += len(bs)
                top_wait()

            def index_scores():
                dve.wait_ge(wi_t, 1)
                nc.vector.tensor_scalar(wi[:], banks[AT["ki"][1] % 8][:, 0:NB * IDX_COLS].rearrange(
                    "p (j c) -> p j c", j=NB)[:, :, WI_AT:WI_AT + IDX_HEADS], IDX_SCALE, None, ALU.mult).then_inc(wi_out, 1)
                dve.wait_ge(wi_out, 1)
                for X in range(8 * (NB - 1)):
                    b, h = X // 8 + 1, X % 8
                    W = (b + 1) * P
                    v = score[:, b - 1, 0:W]
                    dve.wait_ge(idx_relu, X + 1)
                    if X:
                        dve.wait_ge(idx_acc, X)
                    if h == 0:
                        nc.vector.tensor_scalar(v, relu[:, X % 2, 0:W], wi[:, b, h:h + 1], None, ALU.mult).then_inc(idx_acc, 1)
                    else:
                        nc.vector.scalar_tensor_tensor(out=v, in0=relu[:, X % 2, 0:W], scalar=wi[:, b, h:h + 1], in1=v,
                                                       op0=ALU.mult, op1=ALU.add).then_inc(idx_acc, 1)
                dve.wait_ge(idx_acc, 8 * (NB - 1))
                for b in range(1, NB):
                    v = score[:, b - 1, b * P:(b + 1) * P]
                    nc.vector.tensor_tensor(v, v, own, ALU.add).then_inc(top_v, 1)
                top_n[0] += NB - 1
                top_wait()

            def mlp(layer):
                u0, t0, g0 = AT[f"mlp{layer}"]
                h0 = layer * QUARTERS * HID

                def quarter(it, last):
                    def sp(j):
                        split(u0 + j, None, it=it, d_it=MLP_UNITS)

                    def low(f):
                        dve.wait_ge(act_hi_done, it * HID + (h0 + f + 1))
                        nc.vector.tensor_tensor(act_lo[:, f, :], tmp_b[:, f % 3, :], act_hi[:, f, :].bitcast(f32),
                                                ALU.subtract).then_inc(act_lo_done, 1)

                    def hidden(f):
                        dve.wait_ge(tile_done, it * MLP_TILES + (t0 + f + 1))
                        nc.vector.tensor_tensor(tmp_a[:, f % 2, :], banks[(t0 + f) % 8][:], rb[:], ALU.mult).then_inc(tile_out, 1)
                        dve.wait_ge(tile_out, it * MLP_TILES + (t0 + f + 1))
                        if not (isinstance(it, int) and it * HID + h0 + f < 3):
                            dve.wait_ge(act_lo_done, it * HID + (h0 + f - 2))
                        nc.vector.scalar_tensor_tensor(out=tmp_b[:, f % 3, :], in0=tmp_a[:, f % 2, :], scalar=0.0,
                                                       in1=tmp_a[:, f % 2, :], op0=ALU.max, op1=ALU.mult).then_inc(relu2, 1)

                    def down(k):
                        dve.wait_ge(tile_done, it * MLP_TILES + (t0 + 8 + k + 1))
                        nc.vector.tensor_tensor(y[:, k, :], y[:, k, :], banks[(t0 + k) % 8][:], ALU.add).then_inc(tile_out, 1)
                    sp(2)
                    for f in range(4):
                        hidden(f)
                        if f % 4:
                            low(f - 1)
                    low(3)
                    sp(3)
                    sp(4)
                    for f in range(4, 8):
                        hidden(f)
                        if f % 4:
                            low(f - 1)
                    low(7)
                    sp(5)
                    sp(6)
                    dve.wait_ge(y_zero, layer + 1)
                    dve.wait_ge(tile_out, it * MLP_TILES + (t0 + 8))
                    for k in range(4):
                        down(k)
                    sp(7)
                    if not (last and layer):
                        sp(8)
                    for k in range(4, 8):
                        down(k)
                    if not last:
                        sp(9)

                quarter(0, False)
                with dve.Fori(1, QUARTERS - 1) as it:
                    quarter(it, False)
                quarter(QUARTERS - 1, True)

            nc.vector.memset(half_neg, -0.5).then_inc(setup_v, 1)
            nc.vector.memset(small[:, 12:13], PI / 2).then_inc(setup_v, 1)
            nc.vector.memset(ceiling, -NEG).then_inc(setup_v, 1)
            nc.vector.memset(v_hi[:].bitcast(f32), 0.0).then_inc(setup_v, 1)
            nc.vector.memset(v_lo[:].bitcast(f32), 0.0).then_inc(setup_v, 1)
            dve.wait_ge(gains_t, 1)
            nc.vector.tensor_copy(gT[:], banks[7][:, 0:DEPTH * 4 * KT]).then_inc(gains_out, 1)
            dve.wait_ge(gains_out, 1)
            for k in range(KT + 1):
                if k < KT:
                    dve.wait_ge(x_t, k + 1)
                    nc.vector.tensor_copy(xT[:, k, :], banks[x_bank(k)][:]).then_inc(x_ready, 1)
                if k:
                    if k == 1:
                        dve.wait_ge(x_ready, 1)
                    feed_lo(0, 0, 0, k - 1)
                if k == 4:
                    split(0, None, heads=True)
            split(1, None, heads=True)
            dve.wait_ge(const_in, 32)
            dve.wait_ge(small_in, 32)
            n = [0]

            def link(ins):
                ins.then_inc(trig_v, 1)
                n[0] += 1
                dve.wait_ge(trig_v, n[0])

            nc.vector.tensor_scalar(neg_sink, sink, -1.0, None, ALU.mult).then_inc(setup_v, 1)
            link(nc.vector.tensor_copy(ang, pos_i[:]))
            link(nc.vector.tensor_scalar(ang, ang, inv_freq, None, ALU.mult))
            link(nc.vector.tensor_scalar(turns, ang, 1.0 / (2 * PI), ROUND, ALU.mult, ALU.add))
            link(nc.vector.tensor_scalar(turns, turns, -ROUND, None, ALU.add))
            for c in TWO_PI_PARTS:
                link(nc.vector.scalar_tensor_tensor(out=ang, in0=turns, scalar=-c, in1=ang, op0=ALU.mult, op1=ALU.add))
            link(nc.vector.tensor_scalar(ang, ang, PI_IN, -PI_IN, ALU.min, ALU.max))
            stats(NORM["in0"])

            for layer in range(DEPTH):
                name = f"in{layer}"
                u0, t0, g0 = AT[name]
                if layer == 0:
                    dve.wait_ge(trig, 3)
                    dve.wait_ge(rb_out, 1)
                    scaled_tables(0)
                else:
                    uk = AT["ki"][0]
                    gap = w_raw[:, uk % 2, 0:KT * IDX_COLS].rearrange("p (k n) -> p k n", k=KT)[:, :, IDX_DIM:WI_AT]
                    nc.vector.memset(gap, 0.0).then_inc(setup_v, 1)
                    split(AT["qi"][0] + 1, None)
                    stats(NORM["qi"])
                    split(uk, None, cols=KT * IDX_COLS)
                    dve.wait_ge(rb_out, 3)
                    scaled_tables(1)
                    for m in range(4):
                        rope_first("qi", m)
                    split(u0, None, heads=True)
                    for m in range(4):
                        rope_second("qi", m)
                        rope_low("qi", m)
                    rope_first("ki", 0)
                    split(u0 + 1, None, heads=True)
                    rope_second("ki", 0)
                    rope_low("ki", 0)
                for g in range(A_IN_GROUPS):
                    tiles = range(4 * g, 4 * g + 4) if g < 2 else range(8, 10)
                    split(u0 + 2 * g + 2, None, heads=g < 1)
                    for m in tiles:
                        rope_first(name, m)
                    if g == 2:
                        for m in range(2):
                            T, V = t0 + 10 + m, V_AT[name] + m
                            R = ROPE_AT[name] + 10 + m
                            dve.wait_ge(tile_done, T + 1)
                            dve.wait_ge(rope_lo, R - 4 + 1)
                            nc.vector.tensor_tensor(roped[:, R % 4, :], banks[T % 8][:], rb[:], ALU.mult).then_inc(v_scaled, 1)
                    split(u0 + 2 * g + 3, None, heads=g < 1)
                    if layer and g == 0:
                        index_scores()
                    for m in tiles:
                        rope_second(name, m)
                        rope_low(name, m)
                        if layer:
                            for _ in range(2 if m < 6 else 1):
                                top_round((1, 2))
                    if g == 2:
                        for m in range(2):
                            dve.wait_ge(v_hi_done, V_AT[name] + m + 1)
                            nc.vector.tensor_tensor(v_place(v_lo, m), banks[(t0 + 10 + m) % 8][:].rearrange(
                                "p (j a c) -> p j a c", j=NB, a=2), v_place(v_hi, m).bitcast(f32), ALU.subtract).then_inc(tile_out, 1)
                if layer:
                    top_mask((1, 2))

                def extra(j):
                    if layer and j < 8:
                        for _ in range(2):
                            top_round((3,))
                        if j == 7:
                            top_mask((3,))
                attention(layer, extra)

                u0, t0, g0 = AT[f"out{layer}"]
                for g in range(OUT_GROUPS):
                    split(u0 + 2 * g + 2, None)
                    for k in range(4 * g, 4 * g + 4):
                        dve.wait_ge(tile_done, t0 + k + 1)
                        nc.vector.tensor_copy(y[:, k, :], banks[(t0 + k) % 8][:]).then_inc(tile_out, 1)
                    if g == 0:
                        split(u0 + 3, None)
                dve.wait_ge(tile_out, t0 + 8)
                stats(NORM[f"post{layer}"])
                update(NORM[f"post{layer}"], 2 * layer + 1, layer, 1, (layer, 2))
                split(u0 + 5, None)
                stats(NORM[f"mlp{layer}"])
                dve.wait_ge(rb_out, 2 * layer + 2)
                mlp(layer)
                dve.wait_ge(tile_out, AT[f"mlp{layer}"][1] + 64)
                stats(NORM[f"mlp_post{layer}"])
                update(NORM[f"mlp_post{layer}"], 2 * layer + 2, layer, 3, (1, 0) if layer == 0 else None)

            for half in range(2):
                for j in range(NB):
                    dve.wait_ge(out_t, half * NB + j + 1)
                    nc.vector.tensor_copy(out_rows[:, j, half * 512:half * 512 + 512], banks[(AT["end"][1] + half * 4 + j) % 8][:]).then_inc(out_v, 1)

        @block.tensor
        def _(pe):
            def three(bank, whi, wlo, xhi, xlo, start, stop):
                nc.tensor.matmul(bank, whi, xhi, start=start, stop=False)
                nc.tensor.matmul(bank, wlo, xhi, start=False, stop=False)
                return nc.tensor.matmul(bank, whi, xlo, start=False, stop=stop)

            def unit(u, t0, h, xs, k_ready, it=0, d_u=0, d_t=0, mid=None):
                slot = u % 2
                hi = w_hi[:, slot, :].rearrange("p (k n) -> p k n", k=4)
                lo = w_lo[:, slot, :].rearrange("p (k n) -> p k n", k=4)
                pe.wait_ge(w_lo_done, it * d_u + (u + 1))
                order = [(k, m) for k in range(4) for m in range(4)] if h == 0 else [(k, m) for m in range(4) for k in range(4)]
                seen = set()
                for n, (k, m) in enumerate(order):
                    kk = 4 * h + k
                    if k not in seen:
                        k_ready(kk)
                        seen.add(k)
                    if h == 0 and k == 0 and t0 + m >= 8:
                        pe.wait_ge(tile_out, it * d_t + (t0 + m - 7))
                    ins = three(banks[(t0 + m) % 8][:], hi[:, k, m * P:(m + 1) * P], lo[:, k, m * P:(m + 1) * P],
                                xs[0][:, kk, :], xs[1][:, kk, :], h == 0 and k == 0, h == 1 and k == 3)
                    if h == 0 and n == 15:
                        ins.then_inc(half_used, 1)
                    if h == 1 and k == 3:
                        ins.then_inc(tile_done, 1)
                    if h == 1 and n in (11, 15) and mid:
                        mid(n == 15)

            def ssq(norm):
                pe.wait_ge(sq_added, (norm + 1) * (KT - 1))
                pe.wait_ge(sq_done, (norm + 1) * KT)
                for j in range(NB):
                    col = banks[ssq_bank(norm)][:, j:j + 1]
                    nc.tensor.matmul(col, sq_sum[:, j * P:(j + 1) * P], ones[:, 0:1], start=True, stop=False)
                    ins = nc.tensor.matmul(col, sq[:, (KT - 1) % 2, j * P:(j + 1) * P], ones[:, 0:1], start=False, stop=True)
                ins.then_inc(ssq_done, 1)

            def spread(norm):
                for j in range(NB):
                    pe.wait_ge(diag_done, NB * norm + j + 1)
                    ins = nc.tensor.matmul(banks[rb_bank(norm)][:, j * P:(j + 1) * P], ones[:], diag[:, j, :], start=True, stop=True)
                ins.then_inc(rb_done, 1)

            def rotate(name, m):
                T, R = AT[name][1] + m, ROPE_AT[name] + m
                rows = IDX_COLS if name == "ki" else P
                pe.wait_ge(raw_out, R + 1)
                nc.tensor.matmul(banks[T % 8][0:rows, :], rot_t[0:rows, 0:rows], raw[0:rows, R % 4, :], start=True, stop=True).then_inc(rot_done, 1)

            def scores(N):
                layer, i, g = STEPS[N]
                kbs = key_blocks(layer, i)
                W, k0 = len(kbs) * P, kbs[0] * P
                p, a = g // 2, g % 2
                rows = slice(64 * a, 64 * a + 64)
                for r in range(GROUP):
                    if N % 16 >= 1:
                        pe.wait_ge(s_masked, 4 * (N - 1) + r + 1)
                    t, qs = 4 * p + r, slice(i * P, (i + 1) * P)
                    ins = three(banks[r][:, 0:W], act_hi[rows, t, qs], act_lo[rows, t, qs],
                                k_hi[rows, p, k0:k0 + W], k_lo[rows, p, k0:k0 + W], True, True)
                    ins.then_inc(s_ready, 1)

            def transposes(N, K):
                layer, i, g = STEPS[N]
                c = K - PT_AT[N]
                if K == PT_AT[N]:
                    pe.wait_ge(p_done, 3 * N + 3)
                    pe.wait_ge(p_last_done, N + 1)
                if K >= 2:
                    pe.wait_ge(pt_lo_done, K - 1)
                for r in range(GROUP):
                    ins = nc.tensor.transpose(banks[4 + K % 2][:, r * P:(r + 1) * P], probs[:, N % 3, r, c * P:(c + 1) * P], ident)
                ins.then_inc(pt_ready, 1)

            def weighted(N, K):
                layer, i, g = STEPS[N]
                kbs = key_blocks(layer, i)
                kb = kbs[K - PT_AT[N]]
                pair = N // 2
                pe.wait_ge(pt_lo_done, K + 1)
                first, last = g % 2 == 0 and kb == kbs[0], g % 2 == 1 and kb == kbs[-1]
                if first and pair >= 2:
                    pe.wait_ge(o_lo_done, pair - 1)
                c = 2 * HD * g + (HD if g % 2 == 0 else 0)
                three(banks[6 + pair % 2][:], v_hi[:, kb, c:c + P], v_lo[:, kb, c:c + P],
                      pt_hi[:, K % PT_PLACES, :], pt_lo[:, K % PT_PLACES, :], first, last).then_inc(pv_done, 1)

            def attention(layer):
                base = 16 * layer
                scores(base)
                for j in range(18):
                    N = base + j
                    for c, K in enumerate(blocks_of(base, j - 2, 0, 4)):
                        for K2 in blocks_of(base, j - 2, 2 + c, 3 + c):
                            transposes(N - 2, K2)
                        weighted(N - 2, K)
                    for K in blocks_of(base, j - 1, 0, 2):
                        transposes(N - 1, K)
                    if j < 15:
                        scores(N + 1)

            def mlp(layer):
                u0, t0, g0 = AT[f"mlp{layer}"]
                h0 = layer * QUARTERS * HID
                n = 2 * layer + 1

                def quarter(it, first):
                    for g in range(2):
                        for h in range(2):
                            def mid(end):
                                (spread if end else ssq)(NORM[f"mlp{layer}"])
                            unit(u0 + 2 * g + h, t0 + 4 * g, h, (in_hi, in_lo),
                                 lambda k: pe.wait_ge(in_lo_done, n * KT + k + 1), it, MLP_UNITS, MLP_TILES,
                                 mid if first and g == 0 and h == 1 else None)
                            if first and g == 0 and h == 1:
                                pe.wait_ge(rb_out, n + 1)
                    for g in range(2):
                        for h in range(2):
                            unit(u0 + 4 + 2 * g + h, t0 + 8 + 4 * g, h, (act_hi, act_lo),
                                 lambda k: pe.wait_ge(act_lo_done, it * HID + (h0 + k + 1)), it, MLP_UNITS, MLP_TILES)

                quarter(0, True)
                with pe.Fori(1, QUARTERS) as it:
                    quarter(it, False)
                ssq(NORM[f"mlp_post{layer}"])
                spread(NORM[f"mlp_post{layer}"])

            pe.wait_ge(const_in, 32)
            nc.tensor.transpose(banks[7][:, 0:DEPTH * 4 * KT], g_rows[:], ident[0:DEPTH * 4 * KT, 0:DEPTH * 4 * KT]).then_inc(gains_t, 1)
            pe.wait_ge(x_in, 16 * NB)
            pe.wait_ge(gains_out, 1)
            for k in range(KT):
                if k >= 4:
                    pe.wait_ge(x_ready, k - 3)
                for j in range(NB):
                    ins = nc.tensor.transpose(banks[x_bank(k)][:, j * P:(j + 1) * P], x_rows[:, j, k * P:(k + 1) * P], ident)
                ins.then_inc(x_t, 1)
            pe.wait_ge(setup_g, 4)

            for layer in range(DEPTH):
                name = f"in{layer}"
                u0, t0, g0 = AT[name]
                n = 2 * layer
                fed = lambda k: pe.wait_ge(in_lo_done, n * KT + k + 1)
                if layer:
                    uq, tq, _ = AT["qi"]
                    uk, tk, _ = AT["ki"]
                    unit(uq, tq, 0, (in_hi, in_lo), fed)
                    unit(uq + 1, tq, 1, (in_hi, in_lo), fed, mid=lambda end: (spread if end else ssq)(NORM["qi"]))
                    pe.wait_ge(rb_out, n + 1)
                    pe.wait_ge(w_lo_done, uk + 1)
                    pe.wait_ge(tile_out, tk - 7)
                    hi = w_hi[:, uk % 2, 0:KT * IDX_COLS].rearrange("p (k n) -> p k n", k=KT)
                    lo = w_lo[:, uk % 2, 0:KT * IDX_COLS].rearrange("p (k n) -> p k n", k=KT)
                    for k in range(KT):
                        ins = three(banks[tk % 8][0:IDX_COLS, :], hi[:, k, :], lo[:, k, :], in_hi[:, k, :], in_lo[:, k, :], k == 0, k == KT - 1)
                    ins.then_inc(tile_done, 1)
                    for m in range(4):
                        rotate("qi", m)
                for g in range(A_IN_GROUPS):
                    unit(u0 + 2 * g, t0 + 4 * g, 0, (in_hi, in_lo), fed)
                    if g == 0 and layer:
                        rotate("ki", 0)
                    elif g:
                        for m in range(4 * g - 4, 4 * g):
                            rotate(name, m)
                    mid = None
                    if g == 0 and layer == 0:
                        mid = lambda end: (spread if end else ssq)(NORM["in0"])
                    unit(u0 + 2 * g + 1, t0 + 4 * g, 1, (in_hi, in_lo), fed, mid=mid)
                    if g == 0 and layer == 0:
                        pe.wait_ge(rb_out, 1)
                    if g == 0 and layer:
                        R = ROPE_AT["ki"]
                        pe.wait_ge(rope_done, R + 1)
                        for j in range(NB):
                            ins = nc.tensor.transpose(banks[tk % 8][:, j * IDX_COLS:(j + 1) * IDX_COLS],
                                                      roped[0:IDX_COLS, R % 4, j * P:(j + 1) * P], ident[0:IDX_COLS, 0:IDX_COLS])
                        ins.then_inc(wi_t, 1)
                        pe.wait_ge(ki_dup, 32)
                        pe.wait_ge(rope_lo, ROPE_AT["in1"])
                        pe.wait_ge(wi_out, 1)
                        for X in range(8 * (NB - 1)):
                            b, hd = X // 8 + 1, X % 8
                            rows = slice(64 * (hd % 2), 64 * (hd % 2) + 64)
                            if X < 4:
                                pe.wait_ge(tile_out, AT["qi"][1] + 5)
                            else:
                                pe.wait_ge(idx_relu, X - 3)
                            W, qs = (b + 1) * P, slice(b * P, (b + 1) * P)
                            three(banks[idx_bank(X)][:, 0:W], act_hi[rows, hd // 2, qs], act_lo[rows, hd // 2, qs],
                                  pt_hi[rows, 0, 0:W], pt_lo[rows, 0, 0:W], True, True).then_inc(idx_ready, 1)
                        pe.wait_ge(idx_relu, 8 * (NB - 1))
                for m in (8, 9):
                    rotate(name, m)
                for m in range(2):
                    R = ROPE_AT[name] + 10 + m
                    pe.wait_ge(v_scaled, V_AT[name] + m + 1)
                    for j in range(NB):
                        ins = nc.tensor.transpose(banks[(t0 + 10 + m) % 8][:, j * P:(j + 1) * P], roped[:, R % 4, j * P:(j + 1) * P], ident)
                    ins.then_inc(vt_done, 1)
                pe.wait_ge(rope_lo, ROPE_AT[name] + 10)
                pe.wait_ge(tile_out, t0 + 12)
                attention(layer)
                u0, t0, g0 = AT[f"out{layer}"]
                pe.wait_ge(o_lo_done, 8 * (layer + 1))
                for g in range(OUT_GROUPS):
                    for h in range(2):
                        unit(u0 + 2 * g + h, t0 + 4 * g, h, (in_hi, in_lo), lambda k: None)
                ssq(NORM[f"post{layer}"])
                spread(NORM[f"post{layer}"])
                mlp(layer)

            for k in range(KT):
                pe.wait_ge(x_ready, 4 * KT + k + 1)
                if k == 0:
                    pe.wait_ge(tile_out, AT["end"][1])
                if k == 4:
                    pe.wait_ge(x_ready, 5 * KT)
                for j in range(NB):
                    ins = nc.tensor.transpose(banks[(AT["end"][1] + (k // 4) * 4 + j) % 8][:, (k % 4) * P:(k % 4 + 1) * P], xT[:, k, j * P:(j + 1) * P], ident)
                    if k % 4 == 3:
                        ins.then_inc(out_t, 1)


def constants():
    import numpy as np

    c = np.zeros((P, 2 * P + 1), np.float32)
    c[:, 0:P] = np.eye(P, dtype=np.float32)
    half = ROT_DIM // 2
    inv = np.float32(500000.0) ** (-np.arange(0, ROT_DIM, 2, dtype=np.float32) / np.float32(ROT_DIM))
    for head in (0, HD):
        for f in range(half):
            c[head + half + f, P + head + f] = -1.0
            c[head + f, P + head + half + f] = 1.0
            c[head + f, 2 * P] = c[head + half + f, 2 * P] = inv[f]
    return c


def kernel(x, positions, norm_gains, w_mlp_up, w_mlp_down, a_w_in, a_w_out, a_sinks, b_w_in, b_w_out):
    import numpy as np
    import concourse.bacc as bacc
    from concourse.bass_utils import run_bass_kernel_spmd

    nc = bacc.Bacc("TRN2", target_bir_lowering=False, num_devices=1, dynamic_dma_scratch_size=1024)
    arrays, args = {}, []
    for name, a, shape in (
        ("x", x, (SEQ, D)), ("positions", positions, (1, SEQ)), ("norm_gains", norm_gains, (DEPTH * 4 * KT, P)),
        ("w_mlp_up", w_mlp_up, (DEPTH, D, FF)), ("w_mlp_down", w_mlp_down, (DEPTH, FF, D)),
        ("a_w_in", a_w_in, (D, QD + 2 * KVD)), ("a_w_out", a_w_out, (QD, D)), ("a_sinks", a_sinks, (1, NH)),
        ("b_w_in", b_w_in, (D, QD + 2 * KVD + IDX_HEADS * IDX_DIM + IDX_DIM + IDX_HEADS)), ("b_w_out", b_w_out, (QD, D)),
        ("consts", constants(), (P, 2 * P + 1)),
    ):
        a = np.ascontiguousarray(a).reshape(shape)
        arrays[f"in_{name}"] = a
        args.append(nc.dram_tensor(f"in_{name}", a.shape, mybir.dt.from_np(a.dtype), kind="ExternalInput").ap())
    out = nc.dram_tensor("out", (SEQ, D), mybir.dt.float32, kind="ExternalOutput").ap()
    hybrid_trunk(nc, *args, out)
    r = run_bass_kernel_spmd(nc, [arrays], core_ids=[0])
    return r.results[0]["out"].reshape(1, SEQ, D)
```

```python
import concourse.bass as bass
from concourse import mybir
from contextlib import ExitStack

P = 128
D, SEQ, DEPTH = 1024, 512, 2
NH, NKV, HD = 16, 4, 64
GROUP = NH // NKV
FF = 4 * D
IDX_HEADS, IDX_DIM = 8, 64
TOPK = min(256, SEQ // 4)
EPS = 1e-6
KT = D // P
NB = SEQ // P
QD, KVD = NH * HD, NKV * HD
SCALE = HD ** -0.5
IDX_SCALE = IDX_HEADS ** -0.5 * IDX_DIM ** -0.5
ROT_DIM = HD // 4
NEG = -1.0e30
TAKEN = -3.0e38

UNIT = 4 * 512
QUARTERS = 4
HID = FF // QUARTERS // P
MLP_UNITS, MLP_TILES, MLP_GROUPS = 8, 16, 4
A_IN_GROUPS, OUT_GROUPS = 3, 2
IDX_COLS = 88
WI_AT = 80

PI = 3.141592653589793
TWO_PI_PARTS = (6.25, 0.033203125, 2 * PI - 6.25 - 0.033203125)
ROUND = 12582912.0
PI_IN = 3.1415925
TRIG_OPS, SETUP_OPS = 8, 6


def counts():
    at, u, t, g = {}, 0, 0, 0
    for name, du, dt, dg in (
        ("in0", 6, 12, 3), ("out0", 4, 8, 2), ("mlp0", 32, 64, 16),
        ("qi", 2, 4, 1), ("ki", 1, 1, 0), ("in1", 6, 12, 3), ("out1", 4, 8, 2), ("mlp1", 32, 64, 16),
        ("end", 0, 0, 0),
    ):
        at[name] = (u, t, g)
        u, t, g = u + du, t + dt, g + dg
    return at


AT = counts()


def key_blocks(layer, i):
    return list(range(i + 1)) if layer else list(range(max(0, i - 1), i + 1))


PT_PLACES = 4

STEPS = [(layer, i, g) for layer in range(2) for i in range(NB) for g in range(NKV)]
PT_AT = [0]
for _l, _i, _g in STEPS:
    PT_AT.append(PT_AT[-1] + len(key_blocks(_l, _i)))


def blocks_of(base, j, first, end):
    if not 0 <= j < 16:
        return []
    return list(range(PT_AT[base + j], PT_AT[base + j + 1]))[first:end]


def rb_bank(norm):
    before_unit = ("in0", "mlp0", "mlp0", "qi", "qi", "mlp1", "mlp1", "end")[norm]
    return (AT[before_unit][1] + (6 if norm in (0, 2, 4, 6) else 4)) % 8


def ssq_bank(norm):
    return (rb_bank(norm) + 1) % 8


def idx_bank(X):
    return (AT["in1"][1] + 4 + X % 4) % 8


def att_bank(layer, n):
    return (AT["out1" if layer else "out0"][1] + n) % 8


def x_bank(k):
    return 4 + k % 4


def hybrid_trunk(nc, x, positions, gains, w_up, w_down, a_in, a_out, sinks, b_in, b_out, consts, out):
    f32, f32r, i32 = mybir.dt.float32, mybir.dt.float32r, mybir.dt.int32
    ALU, ACT = mybir.AluOpType, mybir.ActivationFunctionType

    ctx = ExitStack()
    with ctx:
        def sb(name, shape, dt=f32):
            return ctx.enter_context(nc.sbuf_tensor(name, shape, dt))

        def sem(name):
            return ctx.enter_context(nc.semaphore(name))

        xT = sb("xT", [P, KT, SEQ])
        in_hi, in_lo = sb("in_hi", [P, KT, SEQ], f32r), sb("in_lo", [P, KT, SEQ], f32r)
        act_hi, act_lo = sb("act_hi", [P, KT, SEQ], f32r), sb("act_lo", [P, KT, SEQ], f32r)
        w_raw = sb("w_raw", [P, 2, UNIT])
        w_hi, w_lo = sb("w_hi", [P, 2, UNIT], f32r), sb("w_lo", [P, 2, UNIT], f32r)
        k_hi, k_lo = sb("k_hi", [P, 2, SEQ], f32r), sb("k_lo", [P, 2, SEQ], f32r)
        v_hi, v_lo = sb("v_hi", [P, NB, 9 * HD], f32r), sb("v_lo", [P, NB, 9 * HD], f32r)
        cos, sin = sb("cos", [P, SEQ]), sb("sin", [P, SEQ])
        cos_r, sin_r = sb("cos_r", [P, SEQ]), sb("sin_r", [P, SEQ])
        rb = sb("rb", [P, SEQ])
        work = sb("work", [P, 7168])
        pt_hi, pt_lo = sb("pt_hi", [P, PT_PLACES, SEQ], f32r), sb("pt_lo", [P, PT_PLACES, SEQ], f32r)
        score = sb("score", [P, NB - 1, SEQ])
        const = sb("const", [P, 2 * P + 1])
        gT = sb("gT", [P, DEPTH * 4 * KT])
        g_rows = sb("g_rows", [DEPTH * 4 * KT, P])
        band = sb("band", [P, 2 * P])
        ones = sb("ones", [P, P])
        diag = sb("diag", [P, NB, P])
        small = sb("small", [P, 128])
        pos_i = sb("pos_i", [P, SEQ], i32)
        banks = [ctx.enter_context(nc.psum_tensor(f"bank{i}", [P, 512], f32)) for i in range(8)]

        ident, rot_t, inv_freq = const[:, 0:P], const[:, P:2 * P], const[:, 2 * P:2 * P + 1]
        own = band[:, P:2 * P]
        x_rows = work[:, 0:NB * D].rearrange("p (j n) -> p j n", j=NB)
        y = work[:, 0:KT * SEQ].rearrange("p (k n) -> p k n", k=KT)
        tmp_a = work[:, 4096:5120].rearrange("p (k n) -> p k n", k=2)
        tmp_b = work[:, 5120:6656].rearrange("p (k n) -> p k n", k=3)
        raw = work[:, 0:2048].rearrange("p (k n) -> p k n", k=4)
        roped = work[:, 2048:4096].rearrange("p (k n) -> p k n", k=4)
        turned = work[:, 4096:5120].rearrange("p (k n) -> p k n", k=2)
        relu = work[:, 5120:6144].rearrange("p (k n) -> p k n", k=2)
        probs = work[:, 0:6144].rearrange("p (s r n) -> p s r n", s=3, r=GROUP)
        out_rows = work[:, 0:NB * D].rearrange("p (j n) -> p j n", j=NB)
        sq = score[:, 0:2, :]
        sq_sum = score[:, 2, :]
        ang, turns, cos_arg = work[:, 4096:4608], work[:, 4608:5120], work[:, 5120:5632]
        ms, rstd, half_neg = small[:, 0:4], small[:, 4:8], small[:, 8:12]
        half_pi = small[:, 12:13]
        ceiling = small[:, 13:14]
        sink = small[:, 16:32]
        neg_sink = small[:, 92:108]
        neg_max = small[:, 44:56].rearrange("p (s r) -> p s r", s=3)
        row_sum = small[:, 56:68].rearrange("p (s r) -> p s r", s=3)
        inv_sum = small[:, 68:80].rearrange("p (s r) -> p s r", s=3)
        sink_e = small[:, 80:92].rearrange("p (s r) -> p s r", s=3)
        top8 = sb("top8", [P, NB - 1, 8])
        wi = sb("wi", [P, NB, IDX_HEADS])

        x_in, const_in, small_in = sem("x_in"), sem("const_in"), sem("small_in")
        w_in = [sem("w_in0"), sem("w_in1")]
        w_hi_done, w_lo_done = sem("w_hi_done"), sem("w_lo_done")
        half_used = sem("half_used")
        tile_done, tile_out = sem("tile_done"), sem("tile_out")
        gains_t, gains_out = sem("gains_t"), sem("gains_out")
        x_t, x_ready = sem("x_t"), sem("x_ready")
        in_hi_done, in_lo_done = sem("in_hi_done"), sem("in_lo_done")
        sq_done, sq_added, sq_zero = sem("sq_done"), sem("sq_added"), sem("sq_zero")
        ssq_done, ms_done, rstd_done = sem("ssq_done"), sem("ms_done"), sem("rstd_done")
        diag_done, rb_done, rb_out = sem("diag_done"), sem("rb_done"), sem("rb_out")
        setup_v, setup_g, trig, trig_v = sem("setup_v"), sem("setup_g"), sem("trig"), sem("trig_v")
        cs_done = sem("cs_done")
        raw_out, rot_done, rope_v, rope_done = sem("raw_out"), sem("rot_done"), sem("rope_v"), sem("rope_done")
        rope_hi, rope_lo = sem("rope_hi"), sem("rope_lo")
        v_scaled = sem("v_scaled")
        vt_done, v_hi_done, v_lo_done = sem("vt_done"), sem("v_hi_done"), sem("v_lo_done")
        ki_dup, wi_t, wi_out = sem("ki_dup"), sem("wi_t"), sem("wi_out")
        idx_ready, idx_relu, idx_acc, top_v = sem("idx_ready"), sem("idx_relu"), sem("idx_acc"), sem("top_v")
        s_ready, s_masked, exp_done, p_last_done = sem("s_ready"), sem("s_masked"), sem("exp_done"), sem("p_last_done")
        sink_d, sink_x, sum_v, inv_done, p_done = (sem("sink_d"), sem("sink_x"), sem("sum_v"),
                                                    sem("inv_done"), sem("p_done"))
        pt_ready, pt_hi_done, pt_lo_done, pv_done = (sem("pt_ready"), sem("pt_hi_done"),
                                                     sem("pt_lo_done"), sem("pv_done"))
        o_hi_done, o_lo_done = sem("o_hi_done"), sem("o_lo_done")
        y_zero, upd = sem("y_zero"), sem("upd")
        relu2, act_hi_done, act_lo_done = sem("relu2"), sem("act_hi_done"), sem("act_lo_done")
        p_mid_done = sem("p_mid_done")
        out_t, out_v, out_in = sem("out_t"), sem("out_v"), sem("out_in")

        block = ctx.enter_context(nc.Block())

        ROPE_AT = {"in0": 0, "qi": 10, "ki": 14, "in1": 15}
        V_AT = {"in0": 0, "in1": 2}
        PRE = {"in0": 0, "mlp0": 1, "qi": 2, "mlp1": 3}
        NORM = {"in0": 0, "post0": 1, "mlp0": 2, "mlp_post0": 3, "qi": 4, "post1": 5, "mlp1": 6, "mlp_post1": 7}

        def rope_place(name, m):
            if name == "ki":
                return pt_hi[:, 0, :], pt_lo[:, 0, :]
            if m >= KT:
                return k_hi[:, m - KT, :], k_lo[:, m - KT, :]
            return act_hi[:, m, :], act_lo[:, m, :]

        def v_place(v, m):
            return v[:, :, HD + 256 * m:HD + 256 * m + 256].rearrange("p j (a c) -> p j a c", c=P)[:, :, :, 0:HD]

        def o_place(t, N):
            _, i, g = STEPS[N]
            p = g // 2
            return t[:, 4 * p:4 * p + 4, i * P:(i + 1) * P]

        def mlp_used(it, j, t0, g0):
            if j % 2 == 0:
                return half_used, it * MLP_GROUPS + (g0 + j // 2 + 1)
            return tile_done, it * MLP_TILES + (t0 + 4 * (j // 2) + 4)

        def gain(layer, n, k):
            c = (layer * 4 + n) * KT + k
            return gT[:, c:c + 1]

        @block.sync
        def _(sp):
            def load(u, src, it=0, d_it=0):
                slot = u % 2
                dst = w_raw[:, slot, :].rearrange("p (k n) -> p k n", k=4)
                if u >= 2:
                    sp.wait_ge(w_lo_done, it * d_it + (u - 1))
                for a in range(2):
                    sp.dma_start(dst[64 * a:64 * a + 64], src(a)).then_inc(w_in[slot], 16)

            def plain(w, row, col):
                v = w[row:row + 512, col:col + 512].rearrange("(k p) n -> p k n", p=P)
                return lambda a: v[64 * a:64 * a + 64]

            for j in range(NB):
                sp.dma_start(x_rows[:, j, :], x[j * P:(j + 1) * P, :]).then_inc(x_in, 16)

            def load_out(name, w):
                u0 = AT[name][0]
                for c in range(OUT_GROUPS):
                    for p in range(2):
                        def src(a):
                            r0 = 512 * p + 256 * a
                            return w[r0:r0 + 256, 512 * c:512 * c + 512].rearrange("(r c) n -> c r n", c=HD)
                        load(u0 + 2 * c + p, src)

            def load_mlp(layer):
                u0 = AT[f"mlp{layer}"][0]

                def quarter(q, it):
                    for j in range(MLP_UNITS):
                        g, h = (j % 4) // 2, j % 2
                        if j < 4:
                            rows, cols = slice(512 * h, 512 * h + 512), bass.ds(q * 1024 + 512 * g, 512)
                            w = w_up[layer]
                        else:
                            rows, cols = bass.ds(q * 1024 + 512 * h, 512), slice(512 * g, 512 * g + 512)
                            w = w_down[layer]
                        v = w[rows, cols].rearrange("(k p) n -> p k n", p=P)
                        load(u0 + j, lambda a: v[64 * a:64 * a + 64], it, MLP_UNITS)
                with sp.Fori(0, QUARTERS) as q:
                    quarter(q, q)

            for g in range(A_IN_GROUPS):
                for h in range(2):
                    load(2 * g + h, plain(a_in, 512 * h, 512 * g))
            load_out("out0", a_out)
            load_mlp(0)
            for h in range(2):
                load(AT["qi"][0] + h, plain(b_in, 512 * h, QD + 2 * KVD))
            u = AT["ki"][0]
            dst = w_raw[:, u % 2, 0:KT * IDX_COLS].rearrange("p (k n) -> p k n", k=KT)
            c0 = QD + 2 * KVD + IDX_HEADS * IDX_DIM
            sp.wait_ge(w_lo_done, u - 1)
            sp.dma_start(dst[:, :, 0:IDX_DIM], b_in[:, c0:c0 + IDX_DIM].rearrange("(k p) n -> p k n", p=P)).then_inc(w_in[u % 2], 16)
            sp.dma_start(dst[:, :, WI_AT:WI_AT + IDX_HEADS],
                         b_in[:, c0 + IDX_DIM:c0 + IDX_DIM + IDX_HEADS].rearrange("(k p) n -> p k n", p=P)).then_inc(w_in[u % 2], 16)
            for g in range(A_IN_GROUPS):
                for h in range(2):
                    load(AT["in1"][0] + 2 * g + h, plain(b_in, 512 * h, 512 * g))
            load_out("out1", b_out)
            load_mlp(1)
            for half in range(2):
                for j in range(NB):
                    sp.wait_ge(out_v, half * NB + j + 1)
                    sp.dma_start(out[j * P:(j + 1) * P, half * 512:half * 512 + 512],
                                 out_rows[:, j, half * 512:half * 512 + 512]).then_inc(out_in, 16)
            sp.wait_ge(out_in, 16 * 2 * NB)

        @block.gpsimd
        def _(pool):
            nc.gpsimd.memset(band[:], 0.0).then_inc(setup_g, 1)
            nc.gpsimd.memset(ones[:], 1.0).then_inc(setup_g, 1)
            pool.wait_ge(setup_g, 1)
            nc.gpsimd.affine_select(out=band[:, 0:P], in_=band[:, 0:P], compare_op=ALU.is_gt, fill=NEG, base=0,
                                    pattern=[[1, P]], channel_multiplier=-1).then_inc(setup_g, 1)
            nc.gpsimd.affine_select(out=band[:, P:2 * P], in_=band[:, P:2 * P], compare_op=ALU.is_ge, fill=NEG, base=0,
                                    pattern=[[-1, P]], channel_multiplier=1).then_inc(setup_g, 1)

            def norm_sums(n):
                if n:
                    pool.wait_ge(ssq_done, n)
                if n == NORM["post1"]:
                    pool.wait_ge(s_masked, 4 * len(STEPS))
                nc.gpsimd.memset(sq_sum, 0.0).then_inc(sq_zero, 1)
                pool.wait_ge(sq_zero, n + 1)
                for k in range(KT - 1):
                    pool.wait_ge(sq_done, n * KT + k + 1)
                    if k:
                        pool.wait_ge(sq_added, n * (KT - 1) + k)
                    nc.gpsimd.tensor_tensor(sq_sum, sq_sum, sq[:, k % 2, :], ALU.add).then_inc(sq_added, 1)
                pool.wait_ge(ms_done, n + 1)
                nc.gpsimd.tensor_tensor(rstd, ms, half_neg, ALU.pow).then_inc(rstd_done, 1)

            def rope_first(name, m):
                R = ROPE_AT[name] + m
                rows = IDX_COLS if name == "ki" else P
                pool.wait_ge(raw_out, R + 1)
                if R >= 4:
                    pool.wait_ge(rope_lo, R - 3)
                if R == ROPE_AT["ki"] + 4:
                    pool.wait_ge(wi_t, 1)
                nc.gpsimd.tensor_tensor(roped[0:rows, R % 4, :], raw[0:rows, R % 4, :], cos_r[0:rows], ALU.mult).then_inc(rope_v, 1)

            def rope_add(name, m):
                R = ROPE_AT[name] + m
                pool.wait_ge(rope_v, R + 1)
                pool.wait_ge(tile_out, AT[name][1] + m + 1)
                nc.gpsimd.tensor_tensor(roped[:, R % 4, :], roped[:, R % 4, :], turned[:, R % 2, :], ALU.add).then_inc(rope_done, 1)

            pool.wait_ge(setup_v, 1)
            for layer in range(DEPTH):
                norm_sums(NORM[("in0", "qi")[layer]])
                pool.wait_ge(cs_done, 2 * layer + 2)
                if layer:
                    for m in range(4):
                        rope_first("qi", m)
                    for m in range(4):
                        rope_add("qi", m)
                    rope_first("ki", 0)
                for g in range(A_IN_GROUPS):
                    for m in range(4 * g, min(4 * g + 4, 10)):
                        rope_first(f"in{layer}", m)
                    if g < 2:
                        for m in range(4 * g, 4 * g + 4):
                            rope_add(f"in{layer}", m)
                for N in range(16 * layer, 16 * layer + 16):
                    pool.wait_ge(inv_done, N + 1)
                    r, W = GROUP - 2, len(key_blocks(*STEPS[N][0:2])) * P
                    v = probs[:, N % 3, r, 0:W]
                    nc.gpsimd.tensor_tensor(v, v, inv_sum[:, N % 3, r:r + 1].to_broadcast([P, W]), ALU.mult).then_inc(p_mid_done, 1)
                norm_sums(NORM[f"post{layer}"])
                norm_sums(NORM[f"mlp{layer}"])
                pool.wait_ge(upd, (2 * layer + 1) * KT)
                nc.gpsimd.memset(y, 0.0).then_inc(y_zero, 1)
                norm_sums(NORM[f"mlp_post{layer}"])

        @block.scalar
        def _(act):
            act.dma_start(const[:], consts).then_inc(const_in, 16)
            act.dma_start(g_rows[:], gains).then_inc(const_in, 16)
            act.dma_start(sink, sinks.broadcast_to([P, NH])).then_inc(small_in, 16)
            act.dma_start(pos_i[:], positions.broadcast_to([P, SEQ])).then_inc(small_in, 16)

            def unit_free(u, done):
                if done is not None:
                    act.wait_ge(*done)

            def split(u, done, heads=False, cols=UNIT, it=0, d_it=0):
                slot = u % 2
                act.wait_ge(w_in[slot], it * (16 * d_it) + 32 * (u // 2 + 1))
                unit_free(u, done)
                if heads:
                    s = w_raw[:, slot, :].rearrange("p (k a r c) -> p k a r c", k=4, a=2, r=4)
                    d = w_hi[:, slot, :].rearrange("p (k r a c) -> p k r a c", k=4, a=2, r=4)
                    for a in range(2):
                        last = nc.scalar.activation(d[:, :, :, a, :], s[:, :, a, :, :], ACT.Copy)
                else:
                    last = nc.scalar.activation(w_hi[:, slot, 0:cols], w_raw[:, slot, 0:cols], ACT.Copy)
                last.then_inc(w_hi_done, 1)

            def feed(n, pre, layer, which, k):
                act.wait_ge(x_ready, n * KT + k + 1)
                nc.scalar.activation(in_hi[:, k, :], xT[:, k, :], ACT.Copy, scale=gain(layer, which, k)).then_inc(in_hi_done, 1)

            def square(norm, src, k):
                if k >= 2:
                    act.wait_ge(sq_added, norm * (KT - 1) + k - 1)
                elif norm:
                    act.wait_ge(ssq_done, norm)
                nc.scalar.activation(sq[:, k % 2, :], src, ACT.Square).then_inc(sq_done, 1)

            def rb_copy(pre, norm):
                act.wait_ge(rb_done, norm + 1)
                nc.scalar.activation(rb[:], banks[rb_bank(norm)][:], ACT.Copy).then_inc(rb_out, 1)

            def copy_raw(name, m):
                T, R = AT[name][1] + m, ROPE_AT[name] + m
                act.wait_ge(tile_done, T + 1)
                if R >= 4:
                    act.wait_ge(rope_done, R - 3)
                rows = IDX_COLS if name == "ki" else P
                nc.scalar.activation(raw[0:rows, R % 4, :], banks[T % 8][0:rows, :], ACT.Copy).then_inc(raw_out, 1)

            def hi_rope(name, m):
                R = ROPE_AT[name] + m
                act.wait_ge(rope_done, R + 1)
                rows = IDX_DIM if name == "ki" else P
                nc.scalar.activation(rope_place(name, m)[0][0:rows], roped[0:rows, R % 4, :], ACT.Copy).then_inc(rope_hi, 1)

            def hi_v(name, m):
                V = V_AT[name] + m
                act.wait_ge(vt_done, V + 1)
                bank = banks[(AT[name][1] + 10 + m) % 8]
                nc.scalar.activation(v_place(v_hi, m), bank[:].rearrange("p (j a c) -> p j a c", j=NB, a=2),
                                     ACT.Copy).then_inc(v_hi_done, 1)

            def expo(N, r):
                layer, i, g = STEPS[N]
                s, W = N % 3, len(key_blocks(layer, i)) * P
                act.wait_ge(s_masked, 4 * N + r + 1)
                nc.scalar.activation(probs[:, s, r, 0:W], probs[:, s, r, 0:W], ACT.Exp,
                                     bias=neg_max[:, s, r:r + 1], scale=-1.0,
                                     accum_out=row_sum[:, s, r:r + 1]).then_inc(exp_done, 1)
                if layer == 0 and r == GROUP - 1:
                    act.wait_ge(sink_d, N + 1)
                    nc.scalar.activation(sink_e[:, s, :], sink_e[:, s, :], ACT.Exp).then_inc(sink_x, 1)

            def normed_last(N):
                layer, i, g = STEPS[N]
                s, W = N % 3, len(key_blocks(layer, i)) * P
                act.wait_ge(inv_done, N + 1)
                nc.scalar.activation(probs[:, s, GROUP - 1, 0:W], probs[:, s, GROUP - 1, 0:W], ACT.Copy,
                                     scale=inv_sum[:, s, GROUP - 1:GROUP]).then_inc(p_last_done, 1)

            def pt_high(K):
                act.wait_ge(pt_ready, K + 1)
                if K >= PT_PLACES:
                    act.wait_ge(pv_done, K - PT_PLACES + 1)
                nc.scalar.activation(pt_hi[:, K % PT_PLACES, :], banks[att_bank(K >= PT_AT[16], 4 + K % 2)][:], ACT.Copy).then_inc(pt_hi_done, 1)

            def o_high(N):
                act.wait_ge(pv_done, PT_AT[N + 1])
                nc.scalar.activation(o_place(in_hi, N), banks[att_bank(N >= 16, 6 + (N // 2) % 2)][:].rearrange("p (r n) -> p r n", r=GROUP),
                                     ACT.Copy).then_inc(o_hi_done, 1)

            def attention(layer):
                base = 16 * layer
                for j in range(19):
                    N = base + j
                    for K in blocks_of(base, j - 2, 2, 4):
                        pt_high(K)
                    if j >= 4 and j % 2 == 0:
                        o_high(N - 3)
                    if 1 <= j < 17:
                        normed_last(N - 1)
                    if j < 16:
                        expo(N, 0)
                        expo(N, 1)
                    for c in range(2):
                        for K in blocks_of(base, j - 1, c, c + 1):
                            pt_high(K)
                        if j < 16:
                            expo(N, 2 + c)

            def mlp(layer):
                u0, t0, g0 = AT[f"mlp{layer}"]

                def quarter(it, last, first=False):
                    def sp(j):
                        split(u0 + j, mlp_used(it, j - 2, t0, g0), it=it, d_it=MLP_UNITS)

                    def hid(fs):
                        for f in fs:
                            act.wait_ge(relu2, it * HID + (layer * QUARTERS * HID + f + 1))
                            nc.scalar.activation(act_hi[:, f, :], tmp_b[:, f % 3, :], ACT.Copy).then_inc(act_hi_done, 1)
                    sp(2)
                    if first:
                        rb_copy(2 * layer + 1, NORM[f"mlp{layer}"])
                    hid(range(0, 2))
                    sp(3)
                    hid(range(2, 4))
                    sp(4)
                    hid(range(4, 8))
                    for j in (5, 6, 7):
                        sp(j)
                    if not (last and layer):
                        sp(8)
                    if not last:
                        sp(9)

                quarter(0, False, first=True)
                with act.Fori(1, QUARTERS - 1) as it:
                    quarter(it, False)
                quarter(QUARTERS - 1, True)
                for k in range(KT):
                    act.wait_ge(tile_out, t0 + MLP_TILES * (QUARTERS - 1) + 8 + k + 1)
                    square(NORM[f"mlp_post{layer}"], y[:, k, :], k)

            def feed_all(name, n, layer, which):
                for k in range(KT):
                    feed(n, PRE[name], layer, which, k)
                    square(NORM[name], xT[:, k, :], k)

            act.wait_ge(gains_out, 1)
            for k in range(KT):
                feed(0, 0, 0, 0, k)
                if k == 1:
                    split(0, None, heads=True)
                if k == 5:
                    split(1, None, heads=True)
                square(NORM["in0"], xT[:, k, :], k)
            act.wait_ge(setup_v, 2)
            act.wait_ge(trig_v, TRIG_OPS)
            nc.scalar.activation(sin[:], ang, ACT.Sin).then_inc(trig, 1)
            nc.scalar.activation(cos_arg, ang, ACT.Abs).then_inc(trig, 1)
            act.wait_ge(trig, 2)
            nc.scalar.activation(cos[:], cos_arg, ACT.Sin, bias=half_pi, scale=-1.0).then_inc(trig, 1)

            for layer in range(DEPTH):
                name = f"in{layer}"
                u0, t0, g0 = AT[name]
                if layer == 0:
                    split(u0 + 2, (half_used, g0 + 1), heads=True)
                    rb_copy(0, NORM["in0"])
                else:
                    uq, tq, gq = AT["qi"]
                    uk, tk, _ = AT["ki"]
                    split(uq + 1, (tile_done, tq))
                    feed_all("qi", 2, 1, 0)
                    act.wait_ge(setup_v, SETUP_OPS + 1)
                    split(uk, (half_used, gq + 1), cols=KT * IDX_COLS)
                    rb_copy(2, NORM["qi"])
                    for m in range(4):
                        copy_raw("qi", m)
                    split(u0, (tile_done, tq + 4), heads=True)
                    split(u0 + 1, (tile_done, tk + 1), heads=True)
                    for m in range(4):
                        hi_rope("qi", m)
                    copy_raw("ki", 0)
                    hi_rope("ki", 0)
                    act.wait_ge(rope_hi, ROPE_AT["ki"] + 1)
                    act.wait_ge(rope_lo, ROPE_AT["ki"] + 1)
                    act.dma_start(pt_hi[64:128, 0, :].bitcast(f32), pt_hi[0:64, 0, :].bitcast(f32)).then_inc(ki_dup, 16)
                    act.dma_start(pt_lo[64:128, 0, :].bitcast(f32), pt_lo[0:64, 0, :].bitcast(f32)).then_inc(ki_dup, 16)
                for g in range(A_IN_GROUPS):
                    if g or layer:
                        split(u0 + 2 * g + 2, (half_used, g0 + g + 1), heads=g < 1)
                    for m in range(4 * g - 4, 4 * g) if g else ():
                        if m == 7:
                            copy_raw(name, 8)
                        hi_rope(name, m)
                    for m in (range(4 * g, 4 * g + 4) if g < 2 else (9,)):
                        copy_raw(name, m)
                    if g == 1 or not layer and g == 0:
                        split(u0 + 2 * g + 3, (tile_done, t0 + 4 * g + 4), heads=g < 1)
                    if layer and g == 0:
                        for X in range(8 * (NB - 1)):
                            if X == 8:
                                split(u0 + 3, (tile_done, t0 + 4), heads=True)
                            W = (X // 8 + 2) * P
                            act.wait_ge(idx_ready, X + 1)
                            if X >= 2:
                                act.wait_ge(idx_acc, X - 1)
                            nc.scalar.activation(relu[:, X % 2, 0:W], banks[idx_bank(X)][:, 0:W], ACT.Relu).then_inc(idx_relu, 1)
                for m in range(2):
                    hi_rope(name, 8 + m)
                for m in range(2):
                    hi_v(name, m)
                attention(layer)
                split(u0 + 7, (tile_done, t0 + 12))
                u0, t0, g0 = AT[f"out{layer}"]
                for g in range(OUT_GROUPS):
                    split(u0 + 2 * g + 2, (half_used, g0 + g + 1))
                    for k in range(4 * g, 4 * g + 4):
                        act.wait_ge(tile_out, t0 + k + 1)
                        square(NORM[f"post{layer}"], y[:, k, :], k)
                    split(u0 + 2 * g + 3, (tile_done, t0 + 4 * g + 4))
                feed_all(f"mlp{layer}", 2 * layer + 1, layer, 2)
                mlp(layer)

        @block.vector
        def _(dve):
            def split(u, done, heads=False, cols=UNIT, it=0, d_it=0):
                slot = u % 2
                dve.wait_ge(w_hi_done, it * d_it + (u + 1))
                if heads:
                    s = w_raw[:, slot, :].rearrange("p (k a r c) -> p k a r c", k=4, a=2, r=4)
                    h = w_hi[:, slot, :].bitcast(f32).rearrange("p (k r a c) -> p k r a c", k=4, a=2, r=4)
                    d = w_lo[:, slot, :].rearrange("p (k r a c) -> p k r a c", k=4, a=2, r=4)
                    for a in range(2):
                        last = nc.vector.tensor_tensor(d[:, :, :, a, :], s[:, :, a, :, :], h[:, :, :, a, :], ALU.subtract)
                else:
                    last = nc.vector.tensor_tensor(w_lo[:, slot, 0:cols], w_raw[:, slot, 0:cols],
                                                   w_hi[:, slot, 0:cols].bitcast(f32), ALU.subtract)
                last.then_inc(w_lo_done, 1)

            def feed_lo(n, layer, which, k):
                dve.wait_ge(in_hi_done, n * KT + k + 1)
                nc.vector.scalar_tensor_tensor(out=in_lo[:, k, :], in0=xT[:, k, :], scalar=gain(layer, which, k),
                                               in1=in_hi[:, k, :].bitcast(f32), op0=ALU.mult,
                                               op1=ALU.subtract).then_inc(in_lo_done, 1)

            def stats(norm):
                dve.wait_ge(ssq_done, norm + 1)
                nc.vector.tensor_scalar(ms, banks[ssq_bank(norm)][:, 0:NB], 1.0 / D, EPS, ALU.mult, ALU.add).then_inc(ms_done, 1)
                dve.wait_ge(rstd_done, norm + 1)
                for j in range(NB):
                    nc.vector.tensor_scalar(diag[:, j, :], ident, rstd[:, j:j + 1], None, ALU.mult).then_inc(diag_done, 1)

            def update(norm, n, layer, which, nxt, u=None):
                dve.wait_ge(rb_done, norm + 1)
                for k in range(KT + 1):
                    if k < KT:
                        if k >= 2:
                            dve.wait_ge(x_ready, n * KT + k - 1)
                        nc.vector.scalar_tensor_tensor(out=tmp_a[:, k % 2, :], in0=y[:, k, :], scalar=gain(layer, which, k),
                                                       in1=banks[rb_bank(norm)][:], op0=ALU.mult, op1=ALU.mult).then_inc(upd, 1)
                    if k and nxt:
                        feed_lo(n, *nxt, k - 1)
                    if k == 4 and nxt:
                        split(u, None)
                    if k < KT:
                        dve.wait_ge(upd, (n - 1) * KT + k + 1)
                        nc.vector.tensor_tensor(xT[:, k, :], xT[:, k, :], tmp_a[:, k % 2, :], ALU.add).then_inc(x_ready, 1)

            def scaled_tables(c):
                nc.vector.tensor_tensor(cos_r[:], cos[:], rb[:], ALU.mult).then_inc(cs_done, 1)
                nc.vector.tensor_tensor(sin_r[:], sin[:], rb[:], ALU.mult).then_inc(cs_done, 1)
                dve.wait_ge(cs_done, 2 * c + 2)

            def rope_turned(name, m):
                T, R = AT[name][1] + m, ROPE_AT[name] + m
                rows = IDX_COLS if name == "ki" else P
                dve.wait_ge(rot_done, R + 1)
                if R >= 2:
                    dve.wait_ge(rope_done, R - 1)
                nc.vector.tensor_tensor(turned[0:rows, R % 2, :], banks[T % 8][0:rows, :], sin_r[0:rows], ALU.mult).then_inc(tile_out, 1)

            def rope_add(name, m):
                R = ROPE_AT[name] + m
                rows = IDX_COLS if name == "ki" else P
                dve.wait_ge(tile_out, AT[name][1] + m + 1)
                dve.wait_ge(rope_v, R + 1)
                nc.vector.tensor_tensor(roped[0:rows, R % 4, :], roped[0:rows, R % 4, :], turned[0:rows, R % 2, :], ALU.add).then_inc(rope_done, 1)

            def rope_low(name, m):
                R = ROPE_AT[name] + m
                rows = IDX_DIM if name == "ki" else P
                hi, lo = rope_place(name, m)
                dve.wait_ge(rope_hi, R + 1)
                nc.vector.tensor_tensor(lo[0:rows], roped[0:rows, R % 4, :], hi[0:rows].bitcast(f32), ALU.subtract).then_inc(rope_lo, 1)

            def rope_tiles(name, ms, between):
                last = None
                for m in ms:
                    rope_turned(name, m)
                    if between and m % 4 in (1, 3):
                        between()
                    if last is not None:
                        rope_low(name, last)
                    last = m
                rope_low(name, last)

            def masked(N, r):
                layer, i, g = STEPS[N]
                s, kbs = N % 3, key_blocks(layer, i)
                W = len(kbs) * P
                dve.wait_ge(s_ready, 4 * N + r + 1)
                if r == 0 and N % 16 >= 3:
                    dve.wait_ge(pt_ready, PT_AT[N - 2])
                if i == 0:
                    mask = own
                elif layer == 0:
                    mask = band[:]
                else:
                    mask = score[:, i - 1, 0:W]
                h = 4 * g + r
                nc.vector.tensor_tensor_reduce(out=probs[:, s, r, 0:W], in0=banks[att_bank(layer, r)][:, 0:W], in1=mask, scale=-SCALE,
                                               scalar=neg_sink[:, h:h + 1] if layer == 0 else ceiling,
                                               op0=ALU.add, op1=ALU.min, accum_out=neg_max[:, s, r:r + 1]).then_inc(s_masked, 1)
                if layer == 0 and r == GROUP - 1:
                    dve.wait_ge(s_masked, 4 * N + 4)
                    nc.vector.tensor_tensor(sink_e[:, s, :], sink[:, 4 * g:4 * g + 4], neg_max[:, s, :], ALU.add).then_inc(sink_d, 1)

            def inverse(N):
                layer, i, g = STEPS[N]
                s = N % 3
                dve.wait_ge(exp_done, 4 * N + 4)
                if layer == 0:
                    dve.wait_ge(sink_x, N + 1)
                    nc.vector.tensor_tensor(row_sum[:, s, :], row_sum[:, s, :], sink_e[:, s, :], ALU.add).then_inc(sum_v, 1)
                    dve.wait_ge(sum_v, N + 1)
                nc.vector.reciprocal(inv_sum[:, s, :], row_sum[:, s, :]).then_inc(inv_done, 1)
                dve.wait_ge(inv_done, N + 1)

            def normed(N, r):
                layer, i, g = STEPS[N]
                s, W = N % 3, len(key_blocks(layer, i)) * P
                nc.vector.tensor_scalar(probs[:, s, r, 0:W], probs[:, s, r, 0:W], inv_sum[:, s, r:r + 1], None, ALU.mult).then_inc(p_done, 1)

            def divided(N):
                inverse(N)
                for r in range(GROUP - 2):
                    normed(N, r)

            def pt_low(K):
                dve.wait_ge(pt_hi_done, K + 1)
                nc.vector.tensor_tensor(pt_lo[:, K % PT_PLACES, :], banks[att_bank(K >= PT_AT[16], 4 + K % 2)][:], pt_hi[:, K % PT_PLACES, :].bitcast(f32),
                                        ALU.subtract).then_inc(pt_lo_done, 1)

            def o_low(N):
                pair = N // 2
                dve.wait_ge(o_hi_done, pair + 1)
                nc.vector.tensor_tensor(o_place(in_lo, N), banks[att_bank(N >= 16, 6 + pair % 2)][:].rearrange("p (r n) -> p r n", r=GROUP),
                                        o_place(in_hi, N).bitcast(f32), ALU.subtract).then_inc(o_lo_done, 1)

            def attention(layer, extra):
                base = 16 * layer
                for j in range(19):
                    N = base + j
                    for K in blocks_of(base, j - 2, 0, 2):
                        pt_low(K)
                    if 1 <= j < 17:
                        divided(N - 1)
                    for c in range(2):
                        if j < 16:
                            masked(N, c)
                        for K in blocks_of(base, j - 2, 2 + c, 3 + c):
                            pt_low(K)
                    if j < 16:
                        masked(N, 2)
                    if j >= 4 and j % 2 == 0:
                        o_low(N - 3)
                    if j < 16:
                        masked(N, 3)
                    extra(j)

            top_n = [0]

            def top_wait():
                dve.wait_ge(top_v, top_n[0])

            def top_round(bs):
                for b in bs:
                    nc.vector.max(top8[:, b - 1, :], score[:, b - 1, 0:(b + 1) * P]).then_inc(top_v, 1)
                top_n[0] += len(bs)
                top_wait()
                for b in bs:
                    v = score[:, b - 1, 0:(b + 1) * P]
                    nc.vector.match_replace(v, top8[:, b - 1, :], v, TAKEN).then_inc(top_v, 1)
                top_n[0] += len(bs)
                top_wait()

            def top_mask(bs):
                for b in bs:
                    v = score[:, b - 1, 0:(b + 1) * P]
                    nc.vector.tensor_scalar(v, v, TAKEN / 2, NEG, ALU.is_gt, ALU.mult).then_inc(top_v, 1)
                top_n[0] += len(bs)
                top_wait()

            def index_scores(u):
                dve.wait_ge(wi_t, 1)
                nc.vector.tensor_scalar(wi[:], banks[AT["ki"][1] % 8][:, 0:NB * IDX_COLS].rearrange(
                    "p (j c) -> p j c", j=NB)[:, :, WI_AT:WI_AT + IDX_HEADS], IDX_SCALE, None, ALU.mult).then_inc(wi_out, 1)
                dve.wait_ge(wi_out, 1)
                for X in range(8 * (NB - 1)):
                    b, h = X // 8 + 1, X % 8
                    W = (b + 1) * P
                    v = score[:, b - 1, 0:W]
                    if X == 8:
                        split(u, None, heads=True)
                    dve.wait_ge(idx_relu, X + 1)
                    if X:
                        dve.wait_ge(idx_acc, X)
                    if h == 0:
                        nc.vector.tensor_scalar(v, relu[:, X % 2, 0:W], wi[:, b, h:h + 1], None, ALU.mult).then_inc(idx_acc, 1)
                    else:
                        nc.vector.scalar_tensor_tensor(out=v, in0=relu[:, X % 2, 0:W], scalar=wi[:, b, h:h + 1], in1=v,
                                                       op0=ALU.mult, op1=ALU.add).then_inc(idx_acc, 1)
                dve.wait_ge(idx_acc, 8 * (NB - 1))
                for b in range(1, NB):
                    v = score[:, b - 1, b * P:(b + 1) * P]
                    nc.vector.tensor_tensor(v, v, own, ALU.add).then_inc(top_v, 1)
                top_n[0] += NB - 1
                top_wait()

            def mlp(layer):
                u0, t0, g0 = AT[f"mlp{layer}"]
                h0 = layer * QUARTERS * HID

                def quarter(it, last, first=False):
                    def sp(j):
                        split(u0 + j, None, it=it, d_it=MLP_UNITS)

                    def low(f):
                        dve.wait_ge(act_hi_done, it * HID + (h0 + f + 1))
                        nc.vector.tensor_tensor(act_lo[:, f, :], tmp_b[:, f % 3, :], act_hi[:, f, :].bitcast(f32),
                                                ALU.subtract).then_inc(act_lo_done, 1)

                    def hidden(f):
                        dve.wait_ge(tile_done, it * MLP_TILES + (t0 + f + 1))
                        nc.vector.tensor_tensor(tmp_a[:, f % 2, :], banks[(t0 + f) % 8][:], rb[:], ALU.mult).then_inc(tile_out, 1)
                        dve.wait_ge(tile_out, it * MLP_TILES + (t0 + f + 1))
                        if not (isinstance(it, int) and it * HID + h0 + f < 3):
                            dve.wait_ge(act_lo_done, it * HID + (h0 + f - 2))
                        nc.vector.scalar_tensor_tensor(out=tmp_b[:, f % 3, :], in0=tmp_a[:, f % 2, :], scalar=0.0,
                                                       in1=tmp_a[:, f % 2, :], op0=ALU.max, op1=ALU.mult).then_inc(relu2, 1)

                    def down(k):
                        dve.wait_ge(tile_done, it * MLP_TILES + (t0 + 8 + k + 1))
                        nc.vector.tensor_tensor(y[:, k, :], y[:, k, :], banks[(t0 + k) % 8][:], ALU.add).then_inc(tile_out, 1)
                    sp(2)
                    if first:
                        stats(NORM[f"mlp{layer}"])
                        dve.wait_ge(rb_out, 2 * layer + 2)
                    for f in range(4):
                        if f == 3:
                            sp(3)
                        hidden(f)
                        if f % 4:
                            low(f - 1)
                    low(3)
                    sp(4)
                    for f in range(4, 8):
                        hidden(f)
                        if f % 4:
                            low(f - 1)
                    low(7)
                    sp(5)
                    sp(6)
                    dve.wait_ge(y_zero, layer + 1)
                    dve.wait_ge(tile_out, it * MLP_TILES + (t0 + 8))
                    for k in range(4):
                        down(k)
                    sp(7)
                    if not (last and layer):
                        sp(8)
                    for k in range(4, 8):
                        down(k)
                    if not last:
                        sp(9)

                quarter(0, False, first=True)
                with dve.Fori(1, QUARTERS - 1) as it:
                    quarter(it, False)
                quarter(QUARTERS - 1, True)

            nc.vector.memset(half_neg, -0.5).then_inc(setup_v, 1)
            nc.vector.memset(small[:, 12:13], PI / 2).then_inc(setup_v, 1)
            nc.vector.memset(ceiling, -NEG).then_inc(setup_v, 1)
            nc.vector.memset(v_hi[:].bitcast(f32), 0.0).then_inc(setup_v, 1)
            nc.vector.memset(v_lo[:].bitcast(f32), 0.0).then_inc(setup_v, 1)
            dve.wait_ge(gains_t, 1)
            nc.vector.tensor_copy(gT[:], banks[7][:, 0:DEPTH * 4 * KT]).then_inc(gains_out, 1)
            dve.wait_ge(gains_out, 1)
            for k in range(KT + 1):
                if k < KT:
                    dve.wait_ge(x_t, k + 1)
                    nc.vector.tensor_copy(xT[:, k, :], banks[x_bank(k)][:]).then_inc(x_ready, 1)
                if k:
                    if k == 1:
                        dve.wait_ge(x_ready, 1)
                    feed_lo(0, 0, 0, k - 1)
                if k == 3:
                    split(0, None, heads=True)
            split(1, None, heads=True)
            dve.wait_ge(const_in, 32)
            dve.wait_ge(small_in, 32)
            n = [0]

            def link(ins):
                ins.then_inc(trig_v, 1)
                n[0] += 1
                dve.wait_ge(trig_v, n[0])

            nc.vector.tensor_scalar(neg_sink, sink, -1.0, None, ALU.mult).then_inc(setup_v, 1)
            link(nc.vector.tensor_copy(ang, pos_i[:]))
            link(nc.vector.tensor_scalar(ang, ang, inv_freq, None, ALU.mult))
            link(nc.vector.tensor_scalar(turns, ang, 1.0 / (2 * PI), ROUND, ALU.mult, ALU.add))
            link(nc.vector.tensor_scalar(turns, turns, -ROUND, None, ALU.add))
            for c in TWO_PI_PARTS:
                link(nc.vector.scalar_tensor_tensor(out=ang, in0=turns, scalar=-c, in1=ang, op0=ALU.mult, op1=ALU.add))
            link(nc.vector.tensor_scalar(ang, ang, PI_IN, -PI_IN, ALU.min, ALU.max))
            for layer in range(DEPTH):
                name = f"in{layer}"
                u0, t0, g0 = AT[name]
                if layer == 0:
                    split(u0 + 2, None, heads=True)
                    stats(NORM["in0"])
                    dve.wait_ge(trig, 3)
                    dve.wait_ge(rb_out, 1)
                    scaled_tables(0)
                else:
                    uk = AT["ki"][0]
                    gap = w_raw[:, uk % 2, 0:KT * IDX_COLS].rearrange("p (k n) -> p k n", k=KT)[:, :, IDX_DIM:WI_AT]
                    nc.vector.memset(gap, 0.0).then_inc(setup_v, 1)
                    split(uk, None, cols=KT * IDX_COLS)
                    stats(NORM["qi"])
                    dve.wait_ge(rb_out, 3)
                    scaled_tables(1)
                    split(u0, None, heads=True)
                    split(u0 + 1, None, heads=True)
                    rope_tiles("qi", range(4), None)
                    rope_turned("ki", 0)
                    rope_add("ki", 0)
                    rope_low("ki", 0)
                between = (lambda: top_round((1, 2))) if layer else None
                if layer:
                    split(u0 + 2, None, heads=True)
                    index_scores(u0 + 3)
                    for _ in range(4):
                        top_round((1, 2, 3))
                else:
                    split(u0 + 3, None, heads=True)
                split(u0 + 4, None)
                rope_tiles(name, range(4), between)
                split(u0 + 5, None)
                if layer:
                    for _ in range(5):
                        top_round((1, 2))
                split(u0 + 6, None)
                rope_tiles(name, range(4, 8), between)

                def scaled_v(m):
                    R = ROPE_AT[name] + 10 + m
                    dve.wait_ge(tile_done, t0 + 10 + m + 1)
                    dve.wait_ge(rope_lo, R - 4 + 1)
                    nc.vector.tensor_tensor(roped[:, R % 4, :], banks[(t0 + 10 + m) % 8][:], rb[:], ALU.mult).then_inc(v_scaled, 1)
                rope_turned(name, 8)
                rope_add(name, 8)
                scaled_v(0)
                rope_low(name, 8)
                rope_turned(name, 9)
                rope_add(name, 9)
                scaled_v(1)
                rope_low(name, 9)
                for m in range(2):
                    dve.wait_ge(v_hi_done, V_AT[name] + m + 1)
                    nc.vector.tensor_tensor(v_place(v_lo, m), banks[(t0 + 10 + m) % 8][:].rearrange(
                        "p (j a c) -> p j a c", j=NB, a=2), v_place(v_hi, m).bitcast(f32), ALU.subtract).then_inc(tile_out, 1)
                dve.wait_ge(rope_lo, ROPE_AT[name] + 10)

                def extra(j):
                    if not layer or j > 11:
                        return
                    top_round((1, 2, 3) if j < 3 else (3,))
                    if j == 3:
                        top_mask((1, 2))
                    if j == 11:
                        top_mask((3,))
                attention(layer, extra)
                split(u0 + 7, None)

                u0, t0, g0 = AT[f"out{layer}"]
                for g in range(OUT_GROUPS):
                    split(u0 + 2 * g + 2, None)
                    for k in range(4 * g, 4 * g + 4):
                        dve.wait_ge(tile_done, t0 + k + 1)
                        nc.vector.tensor_copy(y[:, k, :], banks[(t0 + k) % 8][:]).then_inc(tile_out, 1)
                    if g == 0:
                        split(u0 + 3, None)
                dve.wait_ge(tile_out, t0 + 8)
                stats(NORM[f"post{layer}"])
                update(NORM[f"post{layer}"], 2 * layer + 1, layer, 1, (layer, 2), u0 + 5)
                mlp(layer)
                dve.wait_ge(tile_out, AT[f"mlp{layer}"][1] + 64)
                stats(NORM[f"mlp_post{layer}"])
                update(NORM[f"mlp_post{layer}"], 2 * layer + 2, layer, 3, (1, 0) if layer == 0 else None,
                       AT["qi"][0] + 1)

            for half in range(2):
                for j in range(NB):
                    dve.wait_ge(out_t, half * NB + j + 1)
                    nc.vector.tensor_copy(out_rows[:, j, half * 512:half * 512 + 512], banks[(AT["end"][1] + half * 4 + j) % 8][:]).then_inc(out_v, 1)

        @block.tensor
        def _(pe):
            def three(bank, whi, wlo, xhi, xlo, start, stop):
                nc.tensor.matmul(bank, whi, xhi, start=start, stop=False)
                nc.tensor.matmul(bank, wlo, xhi, start=False, stop=False)
                return nc.tensor.matmul(bank, whi, xlo, start=False, stop=stop)

            def unit(u, t0, h, xs, k_ready, it=0, d_u=0, d_t=0, fresh=False, before={}, after={}):
                slot = u % 2
                hi = w_hi[:, slot, :].rearrange("p (k n) -> p k n", k=4)
                lo = w_lo[:, slot, :].rearrange("p (k n) -> p k n", k=4)
                pe.wait_ge(w_lo_done, it * d_u + (u + 1))
                first_ks = 0 if not fresh else 4 if h == 0 else 2
                order = [(k, m) for k in range(first_ks) for m in range(4)]
                order += [(k, m) for m in range(4) for k in range(first_ks, 4)]
                seen = set()
                for n, (k, m) in enumerate(order):
                    kk = 4 * h + k
                    if k not in seen:
                        k_ready(kk)
                        seen.add(k)
                    if k == 0 and m in before:
                        before[m]()
                    if h == 0 and k == 0 and t0 + m >= 8:
                        pe.wait_ge(tile_out, it * d_t + (t0 + m - 7))
                    ins = three(banks[(t0 + m) % 8][:], hi[:, k, m * P:(m + 1) * P], lo[:, k, m * P:(m + 1) * P],
                                xs[0][:, kk, :], xs[1][:, kk, :], h == 0 and k == 0, h == 1 and k == 3)
                    if h == 0 and n == 15:
                        ins.then_inc(half_used, 1)
                    if h == 1 and k == 3:
                        ins.then_inc(tile_done, 1)
                    if k == 3 and m in after:
                        after[m]()

            def ssq(norm):
                pe.wait_ge(sq_added, (norm + 1) * (KT - 1))
                pe.wait_ge(sq_done, (norm + 1) * KT)
                for j in range(NB):
                    col = banks[ssq_bank(norm)][:, j:j + 1]
                    nc.tensor.matmul(col, sq_sum[:, j * P:(j + 1) * P], ones[:, 0:1], start=True, stop=False)
                    ins = nc.tensor.matmul(col, sq[:, (KT - 1) % 2, j * P:(j + 1) * P], ones[:, 0:1], start=False, stop=True)
                ins.then_inc(ssq_done, 1)

            def spread(norm):
                for j in range(NB):
                    pe.wait_ge(diag_done, NB * norm + j + 1)
                    ins = nc.tensor.matmul(banks[rb_bank(norm)][:, j * P:(j + 1) * P], ones[:], diag[:, j, :], start=True, stop=True)
                ins.then_inc(rb_done, 1)

            def stay_warm(bank, n):
                for _ in range(n):
                    nc.tensor.matmul(bank[:, 0:P], ones[:], ident, start=True, stop=True)

            def post_norm(norm, bank):
                stay_warm(bank, 8)
                ssq(norm)
                stay_warm(bank, 9)
                spread(norm)
                stay_warm(bank, 14)

            def norm_steps(norm):
                return {1: lambda: ssq(norm)}, {0: lambda: spread(norm)}

            def rotate(name, m):
                T, R = AT[name][1] + m, ROPE_AT[name] + m
                rows = IDX_COLS if name == "ki" else P
                pe.wait_ge(raw_out, R + 1)
                nc.tensor.matmul(banks[T % 8][0:rows, :], rot_t[0:rows, 0:rows], raw[0:rows, R % 4, :], start=True, stop=True).then_inc(rot_done, 1)

            def scores(N):
                layer, i, g = STEPS[N]
                kbs = key_blocks(layer, i)
                W, k0 = len(kbs) * P, kbs[0] * P
                p, a = g // 2, g % 2
                rows = slice(64 * a, 64 * a + 64)
                if i == 0 and a == 0:
                    pe.wait_ge(rope_lo, ROPE_AT[f"in{layer}"] + 9 + p)
                for r in range(GROUP):
                    if N % 16 >= 1:
                        pe.wait_ge(s_masked, 4 * (N - 1) + r + 1)
                    t, qs = 4 * p + r, slice(i * P, (i + 1) * P)
                    ins = three(banks[att_bank(layer, r)][:, 0:W], act_hi[rows, t, qs], act_lo[rows, t, qs],
                                k_hi[rows, p, k0:k0 + W], k_lo[rows, p, k0:k0 + W], True, True)
                    ins.then_inc(s_ready, 1)

            def transposes(N, K):
                layer, i, g = STEPS[N]
                c = K - PT_AT[N]
                if K == PT_AT[N]:
                    pe.wait_ge(p_done, 2 * N + 2)
                    pe.wait_ge(p_mid_done, N + 1)
                    pe.wait_ge(p_last_done, N + 1)
                if K - PT_AT[16 * layer] < 2:
                    pe.wait_ge(tile_out, AT[f"in{layer}"][1] + 9 + K - PT_AT[16 * layer])
                if K >= 2:
                    pe.wait_ge(pt_lo_done, K - 1)
                for r in range(GROUP):
                    ins = nc.tensor.transpose(banks[att_bank(layer, 4 + K % 2)][:, r * P:(r + 1) * P], probs[:, N % 3, r, c * P:(c + 1) * P], ident)
                ins.then_inc(pt_ready, 1)

            def weighted(N, K):
                layer, i, g = STEPS[N]
                kbs = key_blocks(layer, i)
                kb = kbs[K - PT_AT[N]]
                pair = N // 2
                pe.wait_ge(pt_lo_done, K + 1)
                first, last = g % 2 == 0 and kb == kbs[0], g % 2 == 1 and kb == kbs[-1]
                if N == 16 * layer:
                    pe.wait_ge(tile_out, AT[f"in{layer}"][1] + 12)
                if first and pair >= 2:
                    pe.wait_ge(o_lo_done, pair - 1)
                c = 2 * HD * g + (HD if g % 2 == 0 else 0)
                three(banks[att_bank(layer, 6 + pair % 2)][:], v_hi[:, kb, c:c + P], v_lo[:, kb, c:c + P],
                      pt_hi[:, K % PT_PLACES, :], pt_lo[:, K % PT_PLACES, :], first, last).then_inc(pv_done, 1)

            def attention(layer):
                base = 16 * layer
                scores(base)
                for j in range(18):
                    N = base + j
                    for c, K in enumerate(blocks_of(base, j - 2, 0, 4)):
                        for K2 in blocks_of(base, j - 2, 2 + c, 3 + c):
                            transposes(N - 2, K2)
                        weighted(N - 2, K)
                    for K in blocks_of(base, j - 1, 0, 2):
                        transposes(N - 1, K)
                    if j < 15:
                        scores(N + 1)

            def mlp(layer):
                u0, t0, g0 = AT[f"mlp{layer}"]
                h0 = layer * QUARTERS * HID
                n = 2 * layer + 1

                def quarter(it, first):
                    for g in range(2):
                        for h in range(2):
                            before, after = {}, {}
                            if first and (g, h) == (0, 1):
                                after = norm_steps(NORM[f"mlp{layer}"])[0]
                            if first and (g, h) == (1, 0):
                                after = norm_steps(NORM[f"mlp{layer}"])[1]
                                before = {2: lambda: pe.wait_ge(rb_out, n + 1)}
                            unit(u0 + 2 * g + h, t0 + 4 * g, h, (in_hi, in_lo),
                                 lambda k: pe.wait_ge(in_lo_done, n * KT + k + 1), it, MLP_UNITS, MLP_TILES,
                                 fresh=first and g == 0, before=before, after=after)
                    for g in range(2):
                        for h in range(2):
                            unit(u0 + 4 + 2 * g + h, t0 + 8 + 4 * g, h, (act_hi, act_lo),
                                 lambda k: pe.wait_ge(act_lo_done, it * HID + (h0 + k + 1)), it, MLP_UNITS, MLP_TILES)

                quarter(0, True)
                with pe.Fori(1, QUARTERS) as it:
                    quarter(it, False)
                post_norm(NORM[f"mlp_post{layer}"], banks[t0 % 8][:])

            pe.wait_ge(const_in, 32)
            nc.tensor.transpose(banks[7][:, 0:DEPTH * 4 * KT], g_rows[:], ident[0:DEPTH * 4 * KT, 0:DEPTH * 4 * KT]).then_inc(gains_t, 1)
            pe.wait_ge(x_in, 16 * NB)
            pe.wait_ge(gains_out, 1)
            for k in range(KT):
                if k >= 4:
                    pe.wait_ge(x_ready, k - 3)
                for j in range(NB):
                    ins = nc.tensor.transpose(banks[x_bank(k)][:, j * P:(j + 1) * P], x_rows[:, j, k * P:(k + 1) * P], ident)
                ins.then_inc(x_t, 1)
            pe.wait_ge(setup_g, 4)

            for layer in range(DEPTH):
                name = f"in{layer}"
                u0, t0, g0 = AT[name]
                n = 2 * layer
                fed = lambda k: pe.wait_ge(in_lo_done, n * KT + k + 1)
                if layer:
                    uq, tq, _ = AT["qi"]
                    uk, tk, _ = AT["ki"]
                    unit(uq, tq, 0, (in_hi, in_lo), fed, fresh=True)
                    unit(uq + 1, tq, 1, (in_hi, in_lo), fed, fresh=True, after=norm_steps(NORM["qi"])[0])
                    pe.wait_ge(w_lo_done, uk + 1)
                    pe.wait_ge(tile_out, tk - 7)
                    hi = w_hi[:, uk % 2, 0:KT * IDX_COLS].rearrange("p (k n) -> p k n", k=KT)
                    lo = w_lo[:, uk % 2, 0:KT * IDX_COLS].rearrange("p (k n) -> p k n", k=KT)
                    for k in range(KT):
                        ins = three(banks[tk % 8][0:IDX_COLS, :], hi[:, k, :], lo[:, k, :], in_hi[:, k, :], in_lo[:, k, :], k == 0, k == KT - 1)
                    ins.then_inc(tile_done, 1)
                    spread(NORM["qi"])
                    for m in range(4):
                        rotate("qi", m)
                for g in range(A_IN_GROUPS):
                    rb_read = {m: lambda: pe.wait_ge(rb_out, n + 1)
                               for m in ((1,) if layer and g == 0 else (2,) if not layer and g == 1 else ())}
                    spread_in0 = norm_steps(NORM["in0"])[1] if not layer and g == 1 else {}
                    unit(u0 + 2 * g, t0 + 4 * g, 0, (in_hi, in_lo), fed, fresh=not layer and g == 0, before=rb_read, after=spread_in0)
                    if g == 0 and layer:
                        rotate("ki", 0)
                    elif g:
                        for m in range(4 * g - 4, 4 * g):
                            rotate(name, m)
                    after = {}
                    if g == 0 and layer == 0:
                        after = norm_steps(NORM["in0"])[0]
                    elif g == 2:
                        after = {2: lambda: rotate(name, 8), 3: lambda: rotate(name, 9)}
                    unit(u0 + 2 * g + 1, t0 + 4 * g, 1, (in_hi, in_lo), fed, fresh=not layer and g == 0, after=after)
                    if g == 0 and layer:
                        R = ROPE_AT["ki"]
                        pe.wait_ge(rope_done, R + 1)
                        for j in range(NB):
                            ins = nc.tensor.transpose(banks[tk % 8][:, j * IDX_COLS:(j + 1) * IDX_COLS],
                                                      roped[0:IDX_COLS, R % 4, j * P:(j + 1) * P], ident[0:IDX_COLS, 0:IDX_COLS])
                        ins.then_inc(wi_t, 1)
                        pe.wait_ge(ki_dup, 32)
                        pe.wait_ge(rope_lo, ROPE_AT["in1"])
                        pe.wait_ge(wi_out, 1)
                        for X in range(8 * (NB - 1)):
                            b, hd = X // 8 + 1, X % 8
                            rows = slice(64 * (hd % 2), 64 * (hd % 2) + 64)
                            if X < 4:
                                pe.wait_ge(tile_out, AT["qi"][1] + 5)
                            else:
                                pe.wait_ge(idx_relu, X - 3)
                            W, qs = (b + 1) * P, slice(b * P, (b + 1) * P)
                            three(banks[idx_bank(X)][:, 0:W], act_hi[rows, hd // 2, qs], act_lo[rows, hd // 2, qs],
                                  pt_hi[rows, 0, 0:W], pt_lo[rows, 0, 0:W], True, True).then_inc(idx_ready, 1)
                        pe.wait_ge(idx_relu, 8 * (NB - 1))
                for m in range(2):
                    R = ROPE_AT[name] + 10 + m
                    pe.wait_ge(v_scaled, V_AT[name] + m + 1)
                    for j in range(NB):
                        ins = nc.tensor.transpose(banks[(t0 + 10 + m) % 8][:, j * P:(j + 1) * P], roped[:, R % 4, j * P:(j + 1) * P], ident)
                    ins.then_inc(vt_done, 1)
                attention(layer)
                u0, t0, g0 = AT[f"out{layer}"]
                pe.wait_ge(o_lo_done, 8 * (layer + 1))
                for g in range(OUT_GROUPS):
                    for h in range(2):
                        unit(u0 + 2 * g + h, t0 + 4 * g, h, (in_hi, in_lo), lambda k: None)
                post_norm(NORM[f"post{layer}"], banks[t0 % 8][:])
                mlp(layer)

            for k in range(KT):
                pe.wait_ge(x_ready, 4 * KT + k + 1)
                if k == 0:
                    pe.wait_ge(tile_out, AT["end"][1])
                if k == 4:
                    pe.wait_ge(x_ready, 5 * KT)
                for j in range(NB):
                    ins = nc.tensor.transpose(banks[(AT["end"][1] + (k // 4) * 4 + j) % 8][:, (k % 4) * P:(k % 4 + 1) * P], xT[:, k, j * P:(j + 1) * P], ident)
                    if k % 4 == 3:
                        ins.then_inc(out_t, 1)


def constants():
    import numpy as np

    c = np.zeros((P, 2 * P + 1), np.float32)
    c[:, 0:P] = np.eye(P, dtype=np.float32)
    half = ROT_DIM // 2
    inv = np.float32(500000.0) ** (-np.arange(0, ROT_DIM, 2, dtype=np.float32) / np.float32(ROT_DIM))
    for head in (0, HD):
        for f in range(half):
            c[head + half + f, P + head + f] = -1.0
            c[head + f, P + head + half + f] = 1.0
            c[head + f, 2 * P] = c[head + half + f, 2 * P] = inv[f]
    return c


def kernel(x, positions, norm_gains, w_mlp_up, w_mlp_down, a_w_in, a_w_out, a_sinks, b_w_in, b_w_out):
    import numpy as np
    import concourse.bacc as bacc
    from concourse.bass_utils import run_bass_kernel_spmd

    nc = bacc.Bacc("TRN2", target_bir_lowering=False, num_devices=1, dynamic_dma_scratch_size=1024)
    arrays, args = {}, []
    for name, a, shape in (
        ("x", x, (SEQ, D)), ("positions", positions, (1, SEQ)), ("norm_gains", norm_gains, (DEPTH * 4 * KT, P)),
        ("w_mlp_up", w_mlp_up, (DEPTH, D, FF)), ("w_mlp_down", w_mlp_down, (DEPTH, FF, D)),
        ("a_w_in", a_w_in, (D, QD + 2 * KVD)), ("a_w_out", a_w_out, (QD, D)), ("a_sinks", a_sinks, (1, NH)),
        ("b_w_in", b_w_in, (D, QD + 2 * KVD + IDX_HEADS * IDX_DIM + IDX_DIM + IDX_HEADS)), ("b_w_out", b_w_out, (QD, D)),
        ("consts", constants(), (P, 2 * P + 1)),
    ):
        a = np.ascontiguousarray(a).reshape(shape)
        arrays[f"in_{name}"] = a
        args.append(nc.dram_tensor(f"in_{name}", a.shape, mybir.dt.from_np(a.dtype), kind="ExternalInput").ap())
    out = nc.dram_tensor("out", (SEQ, D), mybir.dt.float32, kind="ExternalOutput").ap()
    hybrid_trunk(nc, *args, out)
    r = run_bass_kernel_spmd(nc, [arrays], core_ids=[0])
    return r.results[0]["out"].reshape(1, SEQ, D)
```

```python
import concourse.bass as bass
from concourse import mybir
from contextlib import ExitStack

P = 128
D, SEQ, DEPTH = 1024, 512, 2
NH, NKV, HD = 16, 4, 64
GROUP = NH // NKV
FF = 4 * D
IDX_HEADS, IDX_DIM = 8, 64
TOPK = min(256, SEQ // 4)
EPS = 1e-6
KT = D // P
NB = SEQ // P
QD, KVD = NH * HD, NKV * HD
SCALE = HD ** -0.5
IDX_SCALE = IDX_HEADS ** -0.5 * IDX_DIM ** -0.5
ROT_DIM = HD // 4
NEG = -1.0e30
TAKEN = -3.0e38

UNIT = 4 * 512
QUARTERS = 4
HID = FF // QUARTERS // P
MLP_UNITS, MLP_TILES, MLP_GROUPS = 8, 16, 4
A_IN_GROUPS, OUT_GROUPS = 3, 2
IDX_COLS = 88
WI_AT = 80

PI = 3.141592653589793
TWO_PI_PARTS = (6.25, 0.033203125, 2 * PI - 6.25 - 0.033203125)
ROUND = 12582912.0
PI_IN = 3.1415925
TRIG_OPS, SETUP_OPS = 8, 5


def counts():
    at, u, t, g = {}, 0, 0, 0
    for name, du, dt, dg in (
        ("in0", 6, 12, 3), ("out0", 4, 8, 2), ("mlp0", 32, 64, 16),
        ("qi", 2, 4, 1), ("ki", 1, 1, 0), ("in1", 6, 12, 3), ("out1", 4, 8, 2), ("mlp1", 32, 64, 16),
        ("end", 0, 0, 0),
    ):
        at[name] = (u, t, g)
        u, t, g = u + du, t + dt, g + dg
    return at


AT = counts()


def key_blocks(layer, i):
    return list(range(i + 1)) if layer else list(range(max(0, i - 1), i + 1))


PT_PLACES = 8

STEPS = [(layer, i, g) for layer in range(2) for i in range(NB) for g in range(NKV)]
PT_AT = [0]
for _l, _i, _g in STEPS:
    PT_AT.append(PT_AT[-1] + len(key_blocks(_l, _i)))


def blocks_of(base, j, first, end):
    if not 0 <= j < 16:
        return []
    return list(range(PT_AT[base + j], PT_AT[base + j + 1]))[first:end]


def rb_bank(norm):
    before_unit = ("in0", "mlp0", "mlp0", "qi", "qi", "mlp1", "mlp1")[norm]
    return (AT[before_unit][1] + (6 if norm in (0, 2, 4, 6) else 4)) % 8


def ssq_bank(norm):
    return (AT["end"][1] + 7) % 8 if norm == 7 else (rb_bank(norm) + 1) % 8


def idx_bank(X):
    return (AT["in1"][1] + 4 + X % 4) % 8


def att_bank(layer, n):
    return (AT["out1" if layer else "out0"][1] + n) % 8


def x_bank(k):
    return 4 + k % 4


def hybrid_trunk(nc, x, positions, gains, w_up, w_down, a_in, a_out, sinks, b_in, b_out, consts, out):
    f32, f32r, i32 = mybir.dt.float32, mybir.dt.float32r, mybir.dt.int32
    ALU, ACT = mybir.AluOpType, mybir.ActivationFunctionType

    ctx = ExitStack()
    with ctx:
        def sb(name, shape, dt=f32):
            return ctx.enter_context(nc.sbuf_tensor(name, shape, dt))

        def sem(name):
            return ctx.enter_context(nc.semaphore(name))

        xT = sb("xT", [P, KT, SEQ])
        in_hi, in_lo = sb("in_hi", [P, KT, SEQ], f32r), sb("in_lo", [P, KT, SEQ], f32r)
        act_hi, act_lo = sb("act_hi", [P, KT, SEQ], f32r), sb("act_lo", [P, KT, SEQ], f32r)
        w_raw = sb("w_raw", [P, 2, UNIT])
        w_hi, w_lo = sb("w_hi", [P, 2, UNIT], f32r), sb("w_lo", [P, 2, UNIT], f32r)
        k_hi, k_lo = sb("k_hi", [P, 2, SEQ], f32r), sb("k_lo", [P, 2, SEQ], f32r)
        values = sb("values", [P, NB, 9 * HD])
        cos, sin = sb("cos", [P, SEQ]), sb("sin", [P, SEQ])
        cos_r, sin_r = sb("cos_r", [P, SEQ]), sb("sin_r", [P, SEQ])
        rb = sb("rb", [P, SEQ])
        work = sb("work", [P, 8192])
        pt = sb("pt", [P, PT_PLACES, SEQ])
        ki_hi, ki_lo = sb("ki_hi", [P, SEQ], f32r), sb("ki_lo", [P, SEQ], f32r)
        score = sb("score", [P, NB - 1, SEQ])
        const = sb("const", [P, 2 * P + 2])
        gT = sb("gT", [P, DEPTH * 4 * KT])
        band = sb("band", [P, 2 * P])
        ones = sb("ones", [P, P])
        small = sb("small", [P, 160])
        banks = [ctx.enter_context(nc.psum_tensor(f"bank{i}", [P, 512], f32)) for i in range(8)]

        ident, swap_t = const[:, 0:P], const[:, P:2 * P]
        sign, inv_freq = const[:, 2 * P:2 * P + 1], const[:, 2 * P + 1:2 * P + 2]
        own = band[:, P:2 * P]
        x_rows = work[:, 0:NB * D].rearrange("p (j n) -> p j n", j=NB)
        y = work[:, 0:KT * SEQ].rearrange("p (k n) -> p k n", k=KT)
        tmp_a = work[:, 4096:5120].rearrange("p (k n) -> p k n", k=2)
        tmp_b = work[:, 5120:6656].rearrange("p (k n) -> p k n", k=3)
        raw = work[:, 0:2048].rearrange("p (k n) -> p k n", k=4)
        roped = work[:, 2048:4096].rearrange("p (k n) -> p k n", k=4)
        turned = work[:, 4096:6144].rearrange("p (k n) -> p k n", k=4)
        relu = work[:, 6144:7168].rearrange("p (k n) -> p k n", k=2)
        probs = work[:].rearrange("p (s r n) -> p s r n", s=4, r=GROUP)
        x_tok = pt[:].rearrange("p k n -> p (k n)").rearrange("p (j n) -> p j n", j=NB)
        out_rows = w_raw[:].rearrange("p k n -> p (k n)").rearrange("p (j n) -> p j n", j=NB)
        y_gain = xT
        diag = work[:, 7168:7680].rearrange("p (j n) -> p j n", j=NB)
        sq = score[:, 0:2, :]
        sq_sum = score[:, 2, :]
        ang, turns, cos_arg = work[:, 4096:4608], work[:, 4608:5120], work[:, 5120:5632]
        pos_i = work[:, 5632:6144].bitcast(i32)
        g_rows = work[0:DEPTH * 4 * KT, 6144:6272]
        ms, rstd, half_neg = small[:, 0:4], small[:, 4:8], small[:, 8:12]
        half_pi = small[:, 12:13]
        ceiling, mean_col = small[:, 13:14], small[:, 14:15]
        sink = small[:, 16:32]
        neg_sink = small[:, 32:48]
        neg_max, row_sum, inv_sum, sink_e = (
            small[:, c:c + 16].rearrange("p (s r) -> p s r", s=4) for c in (48, 64, 80, 96))
        top8 = sb("top8", [P, NB - 1, 8])
        wi = sb("wi", [P, NB, IDX_HEADS])

        x_in, const_in, small_in = sem("x_in"), sem("const_in"), sem("small_in")
        w_in = [sem("w_in0"), sem("w_in1")]
        w_hi_done, w_lo_done = sem("w_hi_done"), sem("w_lo_done")
        half_used = sem("half_used")
        tile_done, tile_out = sem("tile_done"), sem("tile_out")
        gains_t, gains_out = sem("gains_t"), sem("gains_out")
        x_t, x_ready = sem("x_t"), sem("x_ready")
        in_hi_done, in_lo_done = sem("in_hi_done"), sem("in_lo_done")
        sq_done, sq_added, sq_zero = sem("sq_done"), sem("sq_added"), sem("sq_zero")
        ssq_done, ms_done, rstd_done = sem("ssq_done"), sem("ms_done"), sem("rstd_done")
        diag_done, rb_done, rb_out = sem("diag_done"), sem("rb_done"), sem("rb_out")
        setup_v, setup_g, trig, trig_v = sem("setup_v"), sem("setup_g"), sem("trig"), sem("trig_v")
        cs_done = sem("cs_done")
        turned_done, rope_v, rope_done = sem("turned_done"), sem("rope_v"), sem("rope_done")
        swapped = [sem("swapped0"), sem("swapped1")]
        turned_zero = sem("turned_zero")
        k_raw, k_swapped = sem("k_raw"), sem("k_swapped")
        rope_hi, rope_lo = sem("rope_hi"), sem("rope_lo")
        v_scaled = sem("v_scaled")
        vt_done = sem("vt_done")
        ki_dup, wi_t, wi_out = sem("ki_dup"), sem("wi_t"), sem("wi_out")
        idx_ready, idx_relu, idx_acc, top_v = sem("idx_ready"), sem("idx_relu"), sem("idx_acc"), sem("top_v")
        s_ready, s_masked, exp_done, p_last_done = sem("s_ready"), sem("s_masked"), sem("exp_done"), sem("p_last_done")
        sink_d, sink_x, sum_v, inv_done, p_done = (sem("sink_d"), sem("sink_x"), sem("sum_v"),
                                                    sem("inv_done"), sem("p_done"))
        pt_ready, pt_out, pv_done = sem("pt_ready"), sem("pt_out"), sem("pv_done")
        o_hi_done, o_lo_done = sem("o_hi_done"), sem("o_lo_done")
        y_zero, upd = sem("y_zero"), sem("upd")
        relu2, act_hi_done, act_lo_done = sem("relu2"), sem("act_hi_done"), sem("act_lo_done")
        p_mid_done = sem("p_mid_done")
        x_tok_t, x_tok_out, y_gained = sem("x_tok_t"), sem("x_tok_out"), sem("y_gained")
        out_t, out_v, out_in = sem("out_t"), sem("out_v"), sem("out_in")

        block = ctx.enter_context(nc.Block())

        ROPE_AT = {"in0": 0, "qi": 10, "ki": 14, "in1": 15}
        V_AT = {"in0": 0, "in1": 2}
        SWAP_AT = {"in0": 0, "qi": 2, "ki": 3, "in1": 4}
        TURN_AT = {"in0": 0, "qi": 8, "ki": 12, "in1": 13}

        def place_free(name, m):
            return ROPE_AT[name] + m - 3 if m >= 4 else ROPE_AT["qi"] + 1 if name == "ki" else ROPE_AT[name]
        NORM = {"in0": 0, "post0": 1, "mlp0": 2, "mlp_post0": 3, "qi": 4, "post1": 5, "mlp1": 6, "mlp_post1": 7}

        def rope_place(name, m):
            if name == "ki":
                return ki_hi[:], ki_lo[:]
            if m >= KT:
                return k_hi[:, m - KT, :], k_lo[:, m - KT, :]
            return act_hi[:, m, :], act_lo[:, m, :]

        def v_place(v, m):
            return v[:, :, HD + 256 * m:HD + 256 * m + 256].rearrange("p j (a c) -> p j a c", c=P)[:, :, :, 0:HD]

        def o_place(t, N):
            _, i, g = STEPS[N]
            p = g // 2
            return t[:, 4 * p:4 * p + 4, i * P:(i + 1) * P]

        def mlp_used(it, j, t0, g0):
            if j % 2 == 0:
                return half_used, it * MLP_GROUPS + (g0 + j // 2 + 1)
            return tile_done, it * MLP_TILES + (t0 + 4 * (j // 2) + 4)

        def gain(layer, n, k):
            c = (layer * 4 + n) * KT + k
            return gT[:, c:c + 1]

        @block.sync
        def _(sp):
            def load(u, src, it=0, d_it=0):
                slot = u % 2
                dst = w_raw[:, slot, :].rearrange("p (k n) -> p k n", k=4)
                if u >= 2:
                    sp.wait_ge(w_lo_done, it * d_it + (u - 1))
                for a in range(2):
                    sp.dma_start(dst[64 * a:64 * a + 64], src(a)).then_inc(w_in[slot], 16)

            def plain(w, row, col):
                v = w[row:row + 512, col:col + 512].rearrange("(k p) n -> p k n", p=P)
                return lambda a: v[64 * a:64 * a + 64]

            for j in range(NB):
                sp.dma_start(x_rows[:, j, :], x[j * P:(j + 1) * P, :]).then_inc(x_in, 16)

            def swap(name, m0, n):
                B, half = SWAP_AT[name] + m0 // 4, ROT_DIM // 2
                sp.wait_ge(tile_out, AT[name][1] + m0 + n)
                sp.wait_ge(turned_zero, 1 if name == "in0" else 2)
                for a in (0, HD):
                    for f, t in ((0, half), (half, 0)):
                        sp.dma_start(turned[a + t:a + t + half, 0:n, :], raw[a + f:a + f + half, 0:n, :]).then_inc(swapped[B % 2], 16)

            def load_out(name, w, after_first):
                u0 = AT[name][0]
                for c in range(OUT_GROUPS):
                    for p in range(2):
                        def src(a):
                            r0 = 512 * p + 256 * a
                            return w[r0:r0 + 256, 512 * c:512 * c + 512].rearrange("(r c) n -> c r n", c=HD)
                        load(u0 + 2 * c + p, src)
                        if (c, p) == (0, 0):
                            after_first()

            def load_mlp(layer):
                u0 = AT[f"mlp{layer}"][0]

                def quarter(q, it):
                    for j in range(MLP_UNITS):
                        g, h = (j % 4) // 2, j % 2
                        if j < 4:
                            rows, cols = slice(512 * h, 512 * h + 512), bass.ds(q * 1024 + 512 * g, 512)
                            w = w_up[layer]
                        else:
                            rows, cols = bass.ds(q * 1024 + 512 * h, 512), slice(512 * g, 512 * g + 512)
                            w = w_down[layer]
                        v = w[rows, cols].rearrange("(k p) n -> p k n", p=P)
                        load(u0 + j, lambda a: v[64 * a:64 * a + 64], it, MLP_UNITS)
                with sp.Fori(0, QUARTERS) as q:
                    quarter(q, q)

            for n in range(2 * A_IN_GROUPS):
                load(n, plain(a_in, 512 * (n % 2), 512 * (n // 2)))
                if n == 4:
                    swap("in0", 0, 4)
            load_out("out0", a_out, lambda: swap("in0", 4, 4))
            load_mlp(0)
            for h in range(2):
                load(AT["qi"][0] + h, plain(b_in, 512 * h, QD + 2 * KVD))
            u = AT["ki"][0]
            dst = w_raw[:, u % 2, 0:KT * IDX_COLS].rearrange("p (k n) -> p k n", k=KT)
            c0 = QD + 2 * KVD + IDX_HEADS * IDX_DIM
            sp.wait_ge(w_lo_done, u - 1)
            sp.dma_start(dst[:, :, 0:IDX_DIM], b_in[:, c0:c0 + IDX_DIM].rearrange("(k p) n -> p k n", p=P)).then_inc(w_in[u % 2], 16)
            sp.dma_start(dst[:, :, WI_AT:WI_AT + IDX_HEADS],
                         b_in[:, c0 + IDX_DIM:c0 + IDX_DIM + IDX_HEADS].rearrange("(k p) n -> p k n", p=P)).then_inc(w_in[u % 2], 16)
            for n in range(2 * A_IN_GROUPS):
                load(AT["in1"][0] + n, plain(b_in, 512 * (n % 2), 512 * (n // 2)))
                if n == 1:
                    swap("qi", 0, 4)
                    swap("ki", 0, 1)
                if n == 4:
                    swap("in1", 0, 4)
            load_out("out1", b_out, lambda: swap("in1", 4, 4))
            load_mlp(1)
            for half in range(2):
                for j in range(NB):
                    sp.wait_ge(out_v, half * NB + j + 1)
                    sp.dma_start(out[j * P:(j + 1) * P, half * 512:half * 512 + 512],
                                 out_rows[:, j, half * 512:half * 512 + 512]).then_inc(out_in, 16)
            sp.wait_ge(out_in, 16 * 2 * NB)

        @block.gpsimd
        def _(pool):
            nc.gpsimd.memset(band[:], 0.0).then_inc(setup_g, 1)
            nc.gpsimd.memset(ones[:], 1.0).then_inc(setup_g, 1)
            nc.gpsimd.memset(mean_col, 1.0 / D).then_inc(setup_g, 1)
            pool.wait_ge(setup_g, 1)
            nc.gpsimd.affine_select(out=band[:, 0:P], in_=band[:, 0:P], compare_op=ALU.is_gt, fill=NEG, base=0,
                                    pattern=[[1, P]], channel_multiplier=-1).then_inc(setup_g, 1)
            nc.gpsimd.affine_select(out=band[:, P:2 * P], in_=band[:, P:2 * P], compare_op=ALU.is_ge, fill=NEG, base=0,
                                    pattern=[[-1, P]], channel_multiplier=1).then_inc(setup_g, 1)

            def norm_sums(n):
                if n:
                    pool.wait_ge(ssq_done, n)
                if n == NORM["post1"]:
                    pool.wait_ge(s_masked, 4 * len(STEPS))
                nc.gpsimd.memset(sq_sum, EPS * D / P).then_inc(sq_zero, 1)
                pool.wait_ge(sq_zero, n + 1)
                for k in range(KT - 1):
                    pool.wait_ge(sq_done, n * KT + k + 1)
                    if k:
                        pool.wait_ge(sq_added, n * (KT - 1) + k)
                    nc.gpsimd.tensor_tensor(sq_sum, sq_sum, sq[:, k % 2, :], ALU.add).then_inc(sq_added, 1)
                pool.wait_ge(ms_done, n + 1)
                nc.gpsimd.tensor_tensor(rstd, ms, half_neg, ALU.pow).then_inc(rstd_done, 1)

            def rope_first(name, m):
                R = ROPE_AT[name] + m
                rows = IDX_COLS if name == "ki" else P
                if m < 8:
                    pool.wait_ge(tile_out, AT[name][1] + m + 1)
                else:
                    pool.wait_ge(k_raw, (2 if name == "in1" else 0) + m - 7)
                if place_free(name, m) > 0:
                    pool.wait_ge(rope_lo, place_free(name, m))
                if R == ROPE_AT["in1"]:
                    pool.wait_ge(wi_t, 1)
                nc.gpsimd.tensor_tensor(roped[0:rows, m % 4, :], raw[0:rows, m % 4, :], cos_r[0:rows], ALU.mult).then_inc(rope_v, 1)

            def rope_add(name, m):
                R, B = ROPE_AT[name] + m, SWAP_AT[name] + m // 4
                if name != "qi":
                    pool.wait_ge(swapped[B % 2], 64 * (B // 2 + 1))
                    v = turned[:, m % 4, :]
                    nc.gpsimd.tensor_tensor(v, v, sin_r[:], ALU.mult).then_inc(turned_done, 1)
                pool.wait_ge(rope_v, R + 1)
                pool.wait_ge(turned_done, TURN_AT[name] + m + 1)
                nc.gpsimd.tensor_tensor(roped[:, m % 4, :], roped[:, m % 4, :], turned[:, m % 4, :], ALU.add).then_inc(rope_done, 1)

            pool.wait_ge(setup_v, 1)
            for layer in range(DEPTH):
                norm_sums(NORM[("in0", "qi")[layer]])
                if layer:
                    pool.wait_ge(upd, 2 * KT * layer)
                    pool.wait_ge(x_ready, KT * (2 * layer + 1))
                else:
                    pool.wait_ge(trig, 3)
                nc.gpsimd.memset(turned, 0.0).then_inc(turned_zero, 1)
                pool.wait_ge(cs_done, 2 * layer + 2)
                if layer:
                    for m in range(4):
                        rope_first("qi", m)
                    for m in range(4):
                        rope_add("qi", m)
                    rope_first("ki", 0)
                for g in range(A_IN_GROUPS):
                    for m in range(4 * g, min(4 * g + 4, 10)):
                        rope_first(f"in{layer}", m)
                    if g < 2:
                        for m in range(4 * g, 4 * g + 4):
                            rope_add(f"in{layer}", m)
                for N in range(16 * layer, 16 * layer + 16):
                    pool.wait_ge(inv_done, N + 1)
                    r, W = GROUP - 2, len(key_blocks(*STEPS[N][0:2])) * P
                    v = probs[:, N % 4, r, 0:W]
                    nc.gpsimd.tensor_tensor(v, v, inv_sum[:, N % 4, r:r + 1].to_broadcast([P, W]), ALU.mult).then_inc(p_mid_done, 1)
                norm_sums(NORM[f"post{layer}"])
                norm_sums(NORM[f"mlp{layer}"])
                pool.wait_ge(upd, (2 * layer + 1) * KT)
                nc.gpsimd.memset(y, 0.0).then_inc(y_zero, 1)
                norm_sums(NORM[f"mlp_post{layer}"])

        @block.scalar
        def _(act):
            act.dma_start(const[:], consts).then_inc(const_in, 16)
            act.dma_start(g_rows, gains).then_inc(const_in, 16)
            act.dma_start(sink, sinks.broadcast_to([P, NH])).then_inc(small_in, 16)
            act.dma_start(pos_i, positions.broadcast_to([P, SEQ])).then_inc(small_in, 16)

            def split(u, done, heads=False, cols=UNIT, it=0, d_it=0):
                slot = u % 2
                act.wait_ge(w_in[slot], it * (16 * d_it) + 32 * (u // 2 + 1))
                if done is not None:
                    act.wait_ge(*done)
                if heads:
                    s = w_raw[:, slot, :].rearrange("p (k a r c) -> p k a r c", k=4, a=2, r=4)
                    d = w_hi[:, slot, :].rearrange("p (k r a c) -> p k r a c", k=4, a=2, r=4)
                    for a in range(2):
                        last = nc.scalar.activation(d[:, :, :, a, :], s[:, :, a, :, :], ACT.Copy)
                else:
                    last = nc.scalar.activation(w_hi[:, slot, 0:cols], w_raw[:, slot, 0:cols], ACT.Copy)
                last.then_inc(w_hi_done, 1)

            def feed(n, layer, which, k):
                act.wait_ge(x_ready, n * KT + k + 1)
                nc.scalar.activation(in_hi[:, k, :], xT[:, k, :], ACT.Copy, scale=gain(layer, which, k)).then_inc(in_hi_done, 1)

            def square(norm, src, k):
                if k >= 2:
                    act.wait_ge(sq_added, norm * (KT - 1) + k - 1)
                elif norm:
                    act.wait_ge(ssq_done, norm)
                nc.scalar.activation(sq[:, k % 2, :], src, ACT.Square).then_inc(sq_done, 1)

            def rb_copy(norm):
                act.wait_ge(rb_done, norm + 1)
                nc.scalar.activation(rb[:], banks[rb_bank(norm)][:], ACT.Copy).then_inc(rb_out, 1)

            def copy_raw(name, m):
                T = AT[name][1] + m
                act.wait_ge(tile_done, T + 1)
                if place_free(name, m) > 0:
                    act.wait_ge(rope_done, place_free(name, m))
                rows = IDX_COLS if name == "ki" else P
                nc.scalar.activation(raw[0:rows, m % 4, :], banks[T % 8][0:rows, :], ACT.Copy).then_inc(tile_out if m < 8 else k_raw, 1)

            def hi_rope(name, m):
                R = ROPE_AT[name] + m
                act.wait_ge(rope_done, R + 1)
                rows = IDX_DIM if name == "ki" else P
                nc.scalar.activation(rope_place(name, m)[0][0:rows], roped[0:rows, m % 4, :], ACT.Copy).then_inc(rope_hi, 1)

            def expo(N, r):
                layer, i, g = STEPS[N]
                s, W = N % 4, len(key_blocks(layer, i)) * P
                act.wait_ge(s_masked, 4 * N + r + 1)
                nc.scalar.activation(probs[:, s, r, 0:W], probs[:, s, r, 0:W], ACT.Exp,
                                     bias=neg_max[:, s, r:r + 1], scale=-1.0,
                                     accum_out=row_sum[:, s, r:r + 1]).then_inc(exp_done, 1)
                if layer == 0 and r == GROUP - 1:
                    act.wait_ge(sink_d, N + 1)
                    nc.scalar.activation(sink_e[:, s, :], sink_e[:, s, :], ACT.Exp).then_inc(sink_x, 1)

            def normed_last(N):
                layer, i, g = STEPS[N]
                s, W = N % 4, len(key_blocks(layer, i)) * P
                act.wait_ge(inv_done, N + 1)
                nc.scalar.activation(probs[:, s, GROUP - 1, 0:W], probs[:, s, GROUP - 1, 0:W], ACT.Copy,
                                     scale=inv_sum[:, s, GROUP - 1:GROUP]).then_inc(p_last_done, 1)

            def pt_copy(K):
                act.wait_ge(pt_ready, K + 1)
                if K >= PT_PLACES:
                    act.wait_ge(pv_done, K - PT_PLACES + 1)
                nc.scalar.activation(pt[:, K % PT_PLACES, :], banks[att_bank(K >= PT_AT[16], 4 + K % 2)][:], ACT.Copy).then_inc(pt_out, 1)

            def o_high(N):
                act.wait_ge(pv_done, PT_AT[N + 1])
                nc.scalar.activation(o_place(in_hi, N), banks[att_bank(N >= 16, 6 + (N // 2) % 2)][:].rearrange("p (r n) -> p r n", r=GROUP),
                                     ACT.Copy).then_inc(o_hi_done, 1)

            def attention(layer):
                base = 16 * layer
                for j in range(20):
                    N = base + j
                    for K in blocks_of(base, j - 3, 2, 4):
                        pt_copy(K)
                    if j >= 5 and j % 2 == 1:
                        o_high(N - 4)
                    if j < 16:
                        expo(N, 0)
                    if 1 <= j < 17:
                        normed_last(N - 1)
                    if j < 16:
                        expo(N, 1)
                    for c in range(2):
                        for K in blocks_of(base, j - 2, c, c + 1):
                            pt_copy(K)
                        if j < 16:
                            expo(N, 2 + c)

            def mlp(layer):
                u0, t0, g0 = AT[f"mlp{layer}"]

                def quarter(it, last, first=False):
                    def sp(j):
                        split(u0 + j, mlp_used(it, j - 2, t0, g0), it=it, d_it=MLP_UNITS)

                    def hid(fs):
                        for f in fs:
                            act.wait_ge(relu2, it * HID + (layer * QUARTERS * HID + f + 1))
                            nc.scalar.activation(act_hi[:, f, :], tmp_b[:, f % 3, :], ACT.Copy).then_inc(act_hi_done, 1)
                    sp(2)
                    if first:
                        rb_copy(NORM[f"mlp{layer}"])
                    hid(range(0, 2))
                    sp(3)
                    hid(range(2, 4))
                    sp(4)
                    hid(range(4, 8))
                    sp(5)
                    sp(6)
                    if last and layer:
                        for n in range(2 * NB):
                            half, j = n // NB, n % NB
                            act.wait_ge(x_tok_t, n + 1)
                            nc.scalar.activation(x_tok[:, j, half * 512:half * 512 + 512],
                                                 banks[(t0 + 4 + j) % 8][:], ACT.Copy).then_inc(x_tok_out, 1)
                    sp(7)
                    if not (last and layer):
                        sp(8)
                    if not last:
                        sp(9)

                quarter(0, False, first=True)
                with act.Fori(1, QUARTERS - 1) as it:
                    quarter(it, False)
                quarter(QUARTERS - 1, True)
                for k in range(KT):
                    act.wait_ge(tile_out, t0 + MLP_TILES * (QUARTERS - 1) + 8 + k + 1)
                    square(NORM[f"mlp_post{layer}"], y[:, k, :], k)
                    if layer:
                        nc.scalar.activation(y_gain[:, k, :], y[:, k, :], ACT.Copy, scale=gain(1, 3, k)).then_inc(y_gained, 1)

            def feed_all(name, n, layer, which):
                for k in range(KT):
                    feed(n, layer, which, k)
                    square(NORM[name], xT[:, k, :], k)

            act.wait_ge(gains_out, 1)
            for k in range(KT):
                feed(0, 0, 0, k)
                if k == 1:
                    split(0, None, heads=True)
                if k == 5:
                    split(1, None, heads=True)
                square(NORM["in0"], xT[:, k, :], k)
            act.wait_ge(setup_v, 2)
            act.wait_ge(trig_v, TRIG_OPS)
            nc.scalar.activation(sin[:], ang, ACT.Sin).then_inc(trig, 1)
            nc.scalar.activation(cos_arg, ang, ACT.Abs).then_inc(trig, 1)
            act.wait_ge(trig, 2)
            nc.scalar.activation(cos[:], cos_arg, ACT.Sin, bias=half_pi, scale=-1.0).then_inc(trig, 1)

            for layer in range(DEPTH):
                name = f"in{layer}"
                u0, t0, g0 = AT[name]
                if layer == 0:
                    split(u0 + 2, (half_used, g0 + 1), heads=True)
                    rb_copy(NORM["in0"])
                else:
                    uq, tq, gq = AT["qi"]
                    uk, tk, _ = AT["ki"]
                    split(uq + 1, (tile_done, tq))
                    feed_all("qi", 2, 1, 0)
                    act.wait_ge(setup_v, SETUP_OPS + 1)
                    split(uk, (half_used, gq + 1), cols=KT * IDX_COLS)
                    for m in range(4):
                        copy_raw("qi", m)
                    split(u0, (tile_done, tq + 4), heads=True)
                    rb_copy(NORM["qi"])
                    split(u0 + 1, (tile_done, tk + 1), heads=True)
                    hi_rope("qi", 0)
                    copy_raw("ki", 0)
                    for m in range(1, 4):
                        hi_rope("qi", m)
                    hi_rope("ki", 0)
                    act.wait_ge(rope_hi, ROPE_AT["ki"] + 1)
                    act.wait_ge(rope_lo, ROPE_AT["ki"] + 1)
                    act.dma_start(ki_hi[64:128].bitcast(f32), ki_hi[0:64].bitcast(f32)).then_inc(ki_dup, 16)
                    act.dma_start(ki_lo[64:128].bitcast(f32), ki_lo[0:64].bitcast(f32)).then_inc(ki_dup, 16)
                for g in range(A_IN_GROUPS):
                    if g or layer:
                        split(u0 + 2 * g + 2, (half_used, g0 + g + 1), heads=g < 1)
                    if g < 2:
                        for m in range(4 * g - 4, 4 * g) if g else ():
                            hi_rope(name, m)
                        for m in range(4 * g, 4 * g + 4):
                            copy_raw(name, m)
                    else:
                        for m in range(4, 8):
                            hi_rope(name, m)
                            if m in (5, 6):
                                copy_raw(name, m + 3)
                    if g == 1 or not layer and g == 0:
                        split(u0 + 2 * g + 3, (tile_done, t0 + 4 * g + 4), heads=g < 1)
                    if layer and g == 0:
                        for X in range(8 * (NB - 1)):
                            if X == 8:
                                split(u0 + 3, (tile_done, t0 + 4), heads=True)
                            W = (X // 8 + 2) * P
                            act.wait_ge(idx_ready, X + 1)
                            if X >= 2:
                                act.wait_ge(idx_acc, X - 1)
                            nc.scalar.activation(relu[:, X % 2, 0:W], banks[idx_bank(X)][:, 0:W], ACT.Relu).then_inc(idx_relu, 1)
                for m in range(2):
                    hi_rope(name, 8 + m)
                attention(layer)
                split(u0 + 7, (tile_done, t0 + 12))
                u0, t0, g0 = AT[f"out{layer}"]
                for g in range(OUT_GROUPS):
                    split(u0 + 2 * g + 2, (half_used, g0 + g + 1))
                    for k in range(4 * g, 4 * g + 4):
                        act.wait_ge(tile_out, t0 + k + 1)
                        square(NORM[f"post{layer}"], y[:, k, :], k)
                    split(u0 + 2 * g + 3, (tile_done, t0 + 4 * g + 4))
                feed_all(f"mlp{layer}", 2 * layer + 1, layer, 2)
                mlp(layer)

        @block.vector
        def _(dve):
            def split(u, heads=False, cols=UNIT, it=0, d_it=0):
                slot = u % 2
                dve.wait_ge(w_hi_done, it * d_it + (u + 1))
                if heads:
                    s = w_raw[:, slot, :].rearrange("p (k a r c) -> p k a r c", k=4, a=2, r=4)
                    h = w_hi[:, slot, :].bitcast(f32).rearrange("p (k r a c) -> p k r a c", k=4, a=2, r=4)
                    d = w_lo[:, slot, :].rearrange("p (k r a c) -> p k r a c", k=4, a=2, r=4)
                    for a in range(2):
                        last = nc.vector.tensor_tensor(d[:, :, :, a, :], s[:, :, a, :, :], h[:, :, :, a, :], ALU.subtract)
                else:
                    last = nc.vector.tensor_tensor(w_lo[:, slot, 0:cols], w_raw[:, slot, 0:cols],
                                                   w_hi[:, slot, 0:cols].bitcast(f32), ALU.subtract)
                last.then_inc(w_lo_done, 1)

            def feed_lo(n, layer, which, k):
                dve.wait_ge(in_hi_done, n * KT + k + 1)
                nc.vector.scalar_tensor_tensor(out=in_lo[:, k, :], in0=xT[:, k, :], scalar=gain(layer, which, k),
                                               in1=in_hi[:, k, :].bitcast(f32), op0=ALU.mult,
                                               op1=ALU.subtract).then_inc(in_lo_done, 1)

            def stats(norm):
                dve.wait_ge(ssq_done, norm + 1)
                nc.vector.tensor_reduce(ms, banks[ssq_bank(norm)][:, 0:2 * NB].rearrange("p (j c) -> p j c", c=2),
                                        mybir.AxisListType.X, ALU.add).then_inc(ms_done, 1)
                dve.wait_ge(rstd_done, norm + 1)
                if norm == NORM["mlp_post1"]:
                    return
                for j in range(NB):
                    nc.vector.tensor_scalar(diag[:, j, :], ident, rstd[:, j:j + 1], None, ALU.mult).then_inc(diag_done, 1)

            def update(norm, n, layer, which, nxt, u):
                dve.wait_ge(rb_done, norm + 1)
                for k in range(KT + 1):
                    if k < KT:
                        if k >= 2:
                            dve.wait_ge(x_ready, n * KT + k - 1)
                        nc.vector.scalar_tensor_tensor(out=tmp_a[:, k % 2, :], in0=y[:, k, :], scalar=gain(layer, which, k),
                                                       in1=banks[rb_bank(norm)][:], op0=ALU.mult, op1=ALU.mult).then_inc(upd, 1)
                    if k:
                        feed_lo(n, *nxt, k - 1)
                    if k == 4:
                        split(u)
                    if k < KT:
                        dve.wait_ge(upd, (n - 1) * KT + k + 1)
                        nc.vector.tensor_tensor(xT[:, k, :], xT[:, k, :], tmp_a[:, k % 2, :], ALU.add).then_inc(x_ready, 1)

            def scaled_tables(c):
                nc.vector.tensor_tensor(cos_r[:], cos[:], rb[:], ALU.mult).then_inc(cs_done, 1)
                nc.vector.scalar_tensor_tensor(out=sin_r[:], in0=sin[:], scalar=sign, in1=rb[:], op0=ALU.mult,
                                               op1=ALU.mult).then_inc(cs_done, 1)
                dve.wait_ge(cs_done, 2 * c + 2)

            def rope_turned(name, m):
                if name in ("qi", "ki"):
                    B, rows = SWAP_AT[name], P if name == "qi" else IDX_COLS
                    dve.wait_ge(swapped[B % 2], 64 * (B // 2 + 1))
                    v = turned[0:rows, m % 4, :]
                    nc.vector.tensor_tensor(v, v, sin_r[0:rows], ALU.mult).then_inc(turned_done, 1)
                    dve.wait_ge(turned_done, TURN_AT[name] + m + 1)
                else:
                    T = AT[name][1] + m
                    dve.wait_ge(k_swapped, (2 if name == "in1" else 0) + m - 7)
                    nc.vector.tensor_tensor(turned[:, m % 4, :], banks[T % 8][:], sin_r[:], ALU.mult).then_inc(tile_out, 1)
                    dve.wait_ge(tile_out, T + 1)

            def rope_add(name, m):
                R = ROPE_AT[name] + m
                rows = IDX_COLS if name == "ki" else P
                dve.wait_ge(rope_v, R + 1)
                nc.vector.tensor_tensor(roped[0:rows, m % 4, :], roped[0:rows, m % 4, :], turned[0:rows, m % 4, :], ALU.add).then_inc(rope_done, 1)

            def rope_low(name, m):
                R = ROPE_AT[name] + m
                rows = IDX_DIM if name == "ki" else P
                hi, lo = rope_place(name, m)
                dve.wait_ge(rope_hi, R + 1)
                nc.vector.tensor_tensor(lo[0:rows], roped[0:rows, m % 4, :], hi[0:rows].bitcast(f32), ALU.subtract).then_inc(rope_lo, 1)

            def rope_lows(name, ms, between=None):
                for m in ms:
                    if between and m % 2:
                        between()
                    rope_low(name, m)

            def masked(N, r):
                layer, i, g = STEPS[N]
                s, kbs = N % 4, key_blocks(layer, i)
                W = len(kbs) * P
                dve.wait_ge(s_ready, 4 * N + r + 1)
                if r == 0 and N % 16 >= 4:
                    dve.wait_ge(pt_ready, PT_AT[N - 3])
                if i == 0:
                    mask = own
                elif layer == 0:
                    mask = band[:]
                else:
                    mask = score[:, i - 1, 0:W]
                h = 4 * g + r
                nc.vector.tensor_tensor_reduce(out=probs[:, s, r, 0:W], in0=banks[att_bank(layer, r)][:, 0:W], in1=mask, scale=-SCALE,
                                               scalar=neg_sink[:, h:h + 1] if layer == 0 else ceiling,
                                               op0=ALU.add, op1=ALU.min, accum_out=neg_max[:, s, r:r + 1]).then_inc(s_masked, 1)
                if layer == 0 and r == GROUP - 1:
                    dve.wait_ge(s_masked, 4 * N + 4)
                    nc.vector.tensor_tensor(sink_e[:, s, :], sink[:, 4 * g:4 * g + 4], neg_max[:, s, :], ALU.add).then_inc(sink_d, 1)

            def inverse(N):
                layer, i, g = STEPS[N]
                s = N % 4
                dve.wait_ge(exp_done, 4 * N + 4)
                if layer == 0:
                    dve.wait_ge(sink_x, N + 1)
                    nc.vector.tensor_tensor(row_sum[:, s, :], row_sum[:, s, :], sink_e[:, s, :], ALU.add).then_inc(sum_v, 1)
                    dve.wait_ge(sum_v, N + 1)
                nc.vector.reciprocal(inv_sum[:, s, :], row_sum[:, s, :]).then_inc(inv_done, 1)
                dve.wait_ge(inv_done, N + 1)

            def normed(N, r):
                layer, i, g = STEPS[N]
                s, W = N % 4, len(key_blocks(layer, i)) * P
                nc.vector.tensor_scalar(probs[:, s, r, 0:W], probs[:, s, r, 0:W], inv_sum[:, s, r:r + 1], None, ALU.mult).then_inc(p_done, 1)

            def divided(N):
                inverse(N)
                for r in range(GROUP - 2):
                    normed(N, r)

            def o_low(N):
                pair = N // 2
                dve.wait_ge(o_hi_done, pair + 1)
                nc.vector.tensor_tensor(o_place(in_lo, N), banks[att_bank(N >= 16, 6 + pair % 2)][:].rearrange("p (r n) -> p r n", r=GROUP),
                                        o_place(in_hi, N).bitcast(f32), ALU.subtract).then_inc(o_lo_done, 1)

            def attention(layer, between_turns):
                base = 16 * layer
                for j in range(20):
                    N = base + j
                    for r in range(GROUP):
                        if r == 2 and 1 <= j < 17:
                            divided(N - 1)
                        if j < 16:
                            masked(N, r)
                    if j >= 5 and j % 2 == 1:
                        o_low(N - 4)
                    between_turns(j)

            top_n = [0]

            def top_wait():
                dve.wait_ge(top_v, top_n[0])

            rounds = {b: 0 for b in range(1, NB)}

            def top_round(bs):
                for b in bs:
                    rounds[b] += 1
                    nc.vector.max(top8[:, b - 1, :], score[:, b - 1, 0:(b + 1) * P]).then_inc(top_v, 1)
                top_n[0] += len(bs)
                top_wait()
                for b in bs:
                    v = score[:, b - 1, 0:(b + 1) * P]
                    nc.vector.match_replace(v, top8[:, b - 1, :], v, TAKEN).then_inc(top_v, 1)
                top_n[0] += len(bs)
                top_wait()

            def top_mask(bs):
                for b in bs:
                    v = score[:, b - 1, 0:(b + 1) * P]
                    nc.vector.tensor_scalar(v, v, TAKEN / 2, NEG, ALU.is_gt, ALU.mult).then_inc(top_v, 1)
                top_n[0] += len(bs)
                top_wait()

            def index_scores(u):
                dve.wait_ge(wi_t, 1)
                nc.vector.tensor_scalar(wi[:], banks[AT["ki"][1] % 8][:, 0:NB * IDX_COLS].rearrange(
                    "p (j c) -> p j c", j=NB)[:, :, WI_AT:WI_AT + IDX_HEADS], IDX_SCALE, None, ALU.mult).then_inc(wi_out, 1)
                dve.wait_ge(wi_out, 1)
                for X in range(8 * (NB - 1)):
                    b, h = X // 8 + 1, X % 8
                    W = (b + 1) * P
                    v = score[:, b - 1, 0:W]
                    if X == 8:
                        split(u, heads=True)
                    dve.wait_ge(idx_relu, X + 1)
                    if X:
                        dve.wait_ge(idx_acc, X)
                    if h == 0:
                        nc.vector.tensor_scalar(v, relu[:, X % 2, 0:W], wi[:, b, h:h + 1], None, ALU.mult).then_inc(idx_acc, 1)
                    else:
                        nc.vector.scalar_tensor_tensor(out=v, in0=relu[:, X % 2, 0:W], scalar=wi[:, b, h:h + 1], in1=v,
                                                       op0=ALU.mult, op1=ALU.add).then_inc(idx_acc, 1)
                dve.wait_ge(idx_acc, 8 * (NB - 1))
                for b in range(1, NB):
                    v = score[:, b - 1, b * P:(b + 1) * P]
                    nc.vector.tensor_tensor(v, v, own, ALU.add).then_inc(top_v, 1)
                top_n[0] += NB - 1
                top_wait()

            def mlp(layer):
                u0, t0, g0 = AT[f"mlp{layer}"]
                h0 = layer * QUARTERS * HID

                def quarter(it, last, first=False):
                    def sp(j):
                        split(u0 + j, it=it, d_it=MLP_UNITS)

                    def low(f):
                        dve.wait_ge(act_hi_done, it * HID + (h0 + f + 1))
                        nc.vector.tensor_tensor(act_lo[:, f, :], tmp_b[:, f % 3, :], act_hi[:, f, :].bitcast(f32),
                                                ALU.subtract).then_inc(act_lo_done, 1)

                    def hidden(f):
                        dve.wait_ge(tile_done, it * MLP_TILES + (t0 + f + 1))
                        nc.vector.tensor_tensor(tmp_a[:, f % 2, :], banks[(t0 + f) % 8][:], rb[:], ALU.mult).then_inc(tile_out, 1)
                        dve.wait_ge(tile_out, it * MLP_TILES + (t0 + f + 1))
                        if not (isinstance(it, int) and it * HID + h0 + f < 3):
                            dve.wait_ge(act_lo_done, it * HID + (h0 + f - 2))
                        nc.vector.scalar_tensor_tensor(out=tmp_b[:, f % 3, :], in0=tmp_a[:, f % 2, :], scalar=0.0,
                                                       in1=tmp_a[:, f % 2, :], op0=ALU.max, op1=ALU.mult).then_inc(relu2, 1)

                    def down(k):
                        dve.wait_ge(tile_done, it * MLP_TILES + (t0 + 8 + k + 1))
                        nc.vector.tensor_tensor(y[:, k, :], y[:, k, :], banks[(t0 + k) % 8][:], ALU.add).then_inc(tile_out, 1)
                    sp(2)
                    if first:
                        stats(NORM[f"mlp{layer}"])
                        dve.wait_ge(rb_out, 2 * layer + 2)
                    for f in range(4):
                        if f == 3:
                            sp(3)
                        hidden(f)
                        if f % 4:
                            low(f - 1)
                    low(3)
                    sp(4)
                    for f in range(4, 8):
                        hidden(f)
                        if f % 4:
                            low(f - 1)
                    low(7)
                    sp(5)
                    sp(6)
                    dve.wait_ge(y_zero, layer + 1)
                    dve.wait_ge(tile_out, it * MLP_TILES + (t0 + 8))
                    for k in range(4):
                        down(k)
                    sp(7)
                    if not (last and layer):
                        sp(8)
                    for k in range(4, 8):
                        down(k)
                    if not last:
                        sp(9)

                quarter(0, False, first=True)
                with dve.Fori(1, QUARTERS - 1) as it:
                    quarter(it, False)
                quarter(QUARTERS - 1, True)

            nc.vector.memset(half_neg, -0.5).then_inc(setup_v, 1)
            nc.vector.memset(small[:, 12:13], PI / 2).then_inc(setup_v, 1)
            nc.vector.memset(ceiling, -NEG).then_inc(setup_v, 1)
            nc.vector.memset(values[:], 0.0).then_inc(setup_v, 1)
            dve.wait_ge(gains_t, 1)
            nc.vector.tensor_copy(gT[:], banks[7][:, 0:DEPTH * 4 * KT]).then_inc(gains_out, 1)
            dve.wait_ge(gains_out, 1)
            for k in range(KT + 1):
                if k < KT:
                    dve.wait_ge(x_t, k + 1)
                    nc.vector.tensor_copy(xT[:, k, :], banks[x_bank(k)][:]).then_inc(x_ready, 1)
                if k:
                    if k == 1:
                        dve.wait_ge(x_ready, 1)
                    feed_lo(0, 0, 0, k - 1)
                if k == 3:
                    split(0, heads=True)
            split(1, heads=True)
            dve.wait_ge(const_in, 32)
            dve.wait_ge(small_in, 32)
            n = [0]

            def link(ins):
                ins.then_inc(trig_v, 1)
                n[0] += 1
                dve.wait_ge(trig_v, n[0])

            nc.vector.tensor_scalar(neg_sink, sink, -1.0, None, ALU.mult).then_inc(setup_v, 1)
            link(nc.vector.tensor_copy(ang, pos_i))
            link(nc.vector.tensor_scalar(ang, ang, inv_freq, None, ALU.mult))
            link(nc.vector.tensor_scalar(turns, ang, 1.0 / (2 * PI), ROUND, ALU.mult, ALU.add))
            link(nc.vector.tensor_scalar(turns, turns, -ROUND, None, ALU.add))
            for c in TWO_PI_PARTS:
                link(nc.vector.scalar_tensor_tensor(out=ang, in0=turns, scalar=-c, in1=ang, op0=ALU.mult, op1=ALU.add))
            link(nc.vector.tensor_scalar(ang, ang, PI_IN, -PI_IN, ALU.min, ALU.max))
            for layer in range(DEPTH):
                name = f"in{layer}"
                u0, t0, g0 = AT[name]
                if layer == 0:
                    split(u0 + 2, heads=True)
                    stats(NORM["in0"])
                    dve.wait_ge(trig, 3)
                    dve.wait_ge(rb_out, 1)
                    scaled_tables(0)
                else:
                    uk = AT["ki"][0]
                    gap = w_raw[:, uk % 2, 0:KT * IDX_COLS].rearrange("p (k n) -> p k n", k=KT)[:, :, IDX_DIM:WI_AT]
                    nc.vector.memset(gap, 0.0).then_inc(setup_v, 1)
                    split(uk, cols=KT * IDX_COLS)
                    stats(NORM["qi"])
                    split(u0, heads=True)
                    dve.wait_ge(rb_out, 3)
                    scaled_tables(1)
                    split(u0 + 1, heads=True)
                    for m in range(4):
                        rope_turned("qi", m)
                    rope_lows("qi", range(4))
                    rope_turned("ki", 0)
                    rope_add("ki", 0)
                    rope_low("ki", 0)
                between = (lambda: top_round((1, 2))) if layer else None
                if layer:
                    split(u0 + 2, heads=True)
                    index_scores(u0 + 3)
                    for _ in range(4):
                        top_round((1, 2, 3))
                else:
                    split(u0 + 3, heads=True)
                split(u0 + 4)
                rope_lows(name, range(4), between)
                split(u0 + 5)
                if layer:
                    for _ in range(5):
                        top_round((1, 2))
                split(u0 + 6)
                rope_lows(name, range(4, 8), between)

                def scaled_v(m):
                    R = ROPE_AT[name] + 10 + m
                    dve.wait_ge(tile_done, t0 + 10 + m + 1)
                    dve.wait_ge(rope_lo, R - 4 + 1)
                    nc.vector.tensor_tensor(roped[:, 2 + m, :], banks[(t0 + 10 + m) % 8][:], rb[:], ALU.mult).then_inc(v_scaled, 1)
                rope_turned(name, 8)
                rope_add(name, 8)
                scaled_v(0)
                rope_low(name, 8)
                rope_turned(name, 9)
                rope_add(name, 9)
                scaled_v(1)
                rope_low(name, 9)
                for m in range(2):
                    dve.wait_ge(vt_done, V_AT[name] + m + 1)
                    nc.vector.tensor_copy(v_place(values, m), banks[(t0 + 10 + m) % 8][:].rearrange(
                        "p (j a c) -> p j a c", j=NB, a=2)).then_inc(tile_out, 1)
                dve.wait_ge(rope_lo, ROPE_AT[name] + 10)

                def more_rounds(j):
                    if not layer or j > 11:
                        return
                    due = [-(-(TOPK // 8 - rounds[2]) // (4 - j)) if j < 4 else 0, -(-(TOPK // 8 - rounds[3]) // (12 - j))]
                    for n in range(max(due)):
                        top_round([b for b in range(1, NB) if n < due[b // 3]])
                    if j == 3:
                        top_mask((1, 2))
                    if j == 11:
                        top_mask((3,))

                attention(layer, more_rounds)
                split(u0 + 7)

                u0, t0, g0 = AT[f"out{layer}"]
                for g in range(OUT_GROUPS):
                    split(u0 + 2 * g + 2)
                    for k in range(4 * g, 4 * g + 4):
                        dve.wait_ge(tile_done, t0 + k + 1)
                        nc.vector.tensor_copy(y[:, k, :], banks[(t0 + k) % 8][:]).then_inc(tile_out, 1)
                    if g == 0:
                        split(u0 + 3)
                dve.wait_ge(tile_out, t0 + 8)
                stats(NORM[f"post{layer}"])
                update(NORM[f"post{layer}"], 2 * layer + 1, layer, 1, (layer, 2), u0 + 5)
                mlp(layer)
                dve.wait_ge(tile_out, AT[f"mlp{layer}"][1] + 64)
                stats(NORM[f"mlp_post{layer}"])
                if layer == 0:
                    update(NORM["mlp_post0"], 2, 0, 3, (1, 0), AT["qi"][0] + 1)

            for half in range(2):
                for j in range(NB):
                    dve.wait_ge(out_t, half * NB + j + 1)
                    if (half, j) == (0, 0):
                        dve.wait_ge(x_tok_out, 2 * NB)
                    cols = slice(half * 512, half * 512 + 512)
                    nc.vector.scalar_tensor_tensor(out=out_rows[:, j, cols], in0=banks[(AT["end"][1] + half * 4 + j) % 8][:],
                                                   scalar=rstd[:, j:j + 1], in1=x_tok[:, j, cols], op0=ALU.mult,
                                                   op1=ALU.add).then_inc(out_v, 1)

        @block.tensor
        def _(pe):
            def three(bank, whi, wlo, xhi, xlo, start, stop):
                nc.tensor.matmul(bank, whi, xhi, start=start, stop=False)
                nc.tensor.matmul(bank, wlo, xhi, start=False, stop=False)
                return nc.tensor.matmul(bank, whi, xlo, start=False, stop=stop)

            def unit(u, t0, h, xs, k_ready, it=0, d_u=0, d_t=0, fresh=False, before={}, after={}):
                slot = u % 2
                hi = w_hi[:, slot, :].rearrange("p (k n) -> p k n", k=4)
                lo = w_lo[:, slot, :].rearrange("p (k n) -> p k n", k=4)
                pe.wait_ge(w_lo_done, it * d_u + (u + 1))
                first_ks = 0 if not fresh else 4 if h == 0 else 2
                order = [(k, m) for k in range(first_ks) for m in range(4)]
                order += [(k, m) for m in range(4) for k in range(first_ks, 4)]
                seen = set()
                for n, (k, m) in enumerate(order):
                    kk = 4 * h + k
                    if k not in seen:
                        k_ready(kk)
                        seen.add(k)
                    if k == 0 and m in before:
                        before[m]()
                    if h == 0 and k == 0 and t0 + m >= 8:
                        pe.wait_ge(tile_out, it * d_t + (t0 + m - 7))
                    ins = three(banks[(t0 + m) % 8][:], hi[:, k, m * P:(m + 1) * P], lo[:, k, m * P:(m + 1) * P],
                                xs[0][:, kk, :], xs[1][:, kk, :], h == 0 and k == 0, h == 1 and k == 3)
                    if h == 0 and n == 15:
                        ins.then_inc(half_used, 1)
                    if h == 1 and k == 3:
                        ins.then_inc(tile_done, 1)
                    if k == 3 and m in after:
                        after[m]()

            def ssq(norm):
                pe.wait_ge(sq_added, (norm + 1) * (KT - 1))
                if norm in (1, 3, 5):
                    pe.wait_ge(sq_done, norm * KT + KT - 1)
                for j in range(NB):
                    nc.tensor.matmul(banks[ssq_bank(norm)][:, 2 * j:2 * j + 1], sq_sum[:, j * P:(j + 1) * P], mean_col,
                                     start=True, stop=True)
                pe.wait_ge(sq_done, (norm + 1) * KT)
                for j in range(NB):
                    ins = nc.tensor.matmul(banks[ssq_bank(norm)][:, 2 * j + 1:2 * j + 2], sq[:, (KT - 1) % 2, j * P:(j + 1) * P],
                                           mean_col, start=True, stop=True)
                ins.then_inc(ssq_done, 1)

            def spread(norm):
                for j in range(NB):
                    pe.wait_ge(diag_done, NB * norm + j + 1)
                    ins = nc.tensor.matmul(banks[rb_bank(norm)][:, j * P:(j + 1) * P], ones[:], diag[:, j, :], start=True, stop=True)
                ins.then_inc(rb_done, 1)

            def stay_warm(bank, n):
                for _ in range(n):
                    nc.tensor.matmul(bank[:, 0:P], ones[:], ident, start=True, stop=True)

            def post_norm(norm, bank):
                stay_warm(bank, 4)
                ssq(norm)
                stay_warm(bank, 6)
                spread(norm)
                stay_warm(bank, 10)

            def norm_steps(norm):
                return {1: lambda: ssq(norm)}, {0: lambda: spread(norm)}

            def scores(N):
                layer, i, g = STEPS[N]
                kbs = key_blocks(layer, i)
                W, k0 = len(kbs) * P, kbs[0] * P
                p, a = g // 2, g % 2
                rows = slice(64 * a, 64 * a + 64)
                if i == 0 and a == 0:
                    pe.wait_ge(rope_lo, ROPE_AT[f"in{layer}"] + 9 + p)
                for r in range(GROUP):
                    if N % 16 >= 1:
                        pe.wait_ge(s_masked, 4 * (N - 1) + r + 1)
                    t, qs = 4 * p + r, slice(i * P, (i + 1) * P)
                    ins = three(banks[att_bank(layer, r)][:, 0:W], act_hi[rows, t, qs], act_lo[rows, t, qs],
                                k_hi[rows, p, k0:k0 + W], k_lo[rows, p, k0:k0 + W], True, True)
                    ins.then_inc(s_ready, 1)

            def transposes(N, K):
                layer, i, g = STEPS[N]
                c = K - PT_AT[N]
                if K == PT_AT[N]:
                    pe.wait_ge(p_done, 2 * N + 2)
                    pe.wait_ge(p_mid_done, N + 1)
                    pe.wait_ge(p_last_done, N + 1)
                if K - PT_AT[16 * layer] < 2:
                    pe.wait_ge(tile_out, AT[f"in{layer}"][1] + 9 + K - PT_AT[16 * layer])
                if K >= 2:
                    pe.wait_ge(pt_out, K - 1)
                for r in range(GROUP):
                    ins = nc.tensor.transpose(banks[att_bank(layer, 4 + K % 2)][:, r * P:(r + 1) * P], probs[:, N % 4, r, c * P:(c + 1) * P], ident)
                ins.then_inc(pt_ready, 1)

            def weighted(N, K):
                layer, i, g = STEPS[N]
                kbs = key_blocks(layer, i)
                kb = kbs[K - PT_AT[N]]
                pair = N // 2
                pe.wait_ge(pt_out, K + 1)
                first, last = g % 2 == 0 and kb == kbs[0], g % 2 == 1 and kb == kbs[-1]
                if N == 16 * layer:
                    pe.wait_ge(tile_out, AT[f"in{layer}"][1] + 12)
                if first and pair >= 2:
                    pe.wait_ge(o_lo_done, pair - 1)
                c = 2 * HD * g + (HD if g % 2 == 0 else 0)
                nc.tensor.matmul(banks[att_bank(layer, 6 + pair % 2)][:], values[:, kb, c:c + P],
                                 pt[:, K % PT_PLACES, :], start=first, stop=last).then_inc(pv_done, 1)

            def attention(layer):
                base = 16 * layer
                scores(base)
                for j in range(19):
                    N = base + j
                    for c, K in enumerate(blocks_of(base, j - 3, 0, 4)):
                        for K2 in blocks_of(base, j - 3, 2 + c, 3 + c):
                            transposes(N - 3, K2)
                        weighted(N - 3, K)
                    for K in blocks_of(base, j - 2, 0, 2):
                        transposes(N - 2, K)
                    if j < 15:
                        scores(N + 1)

            def mlp(layer):
                u0, t0, g0 = AT[f"mlp{layer}"]
                h0 = layer * QUARTERS * HID
                n = 2 * layer + 1

                def x_tokens(half):
                    if half:
                        pe.wait_ge(x_tok_out, NB)
                    else:
                        pe.wait_ge(tile_out, t0 + (QUARTERS - 1) * MLP_TILES + 8)
                    for j in range(NB):
                        for k in range(4):
                            ins = nc.tensor.transpose(banks[(t0 + 4 + j) % 8][:, k * P:(k + 1) * P],
                                                      xT[:, 4 * half + k, j * P:(j + 1) * P], ident)
                        ins.then_inc(x_tok_t, 1)

                def quarter(it, first, end=False):
                    for g in range(2):
                        for h in range(2):
                            before, after = {}, {}
                            if first and (g, h) == (0, 1):
                                after = norm_steps(NORM[f"mlp{layer}"])[0]
                            if first and (g, h) == (1, 0):
                                after = norm_steps(NORM[f"mlp{layer}"])[1]
                                before = {2: lambda: pe.wait_ge(rb_out, n + 1)}
                            unit(u0 + 2 * g + h, t0 + 4 * g, h, (in_hi, in_lo),
                                 lambda k: pe.wait_ge(in_lo_done, n * KT + k + 1), it, MLP_UNITS, MLP_TILES,
                                 fresh=first and g == 0, before=before, after=after)
                    for g in range(2):
                        for h in range(2):
                            before, after = {}, {}
                            if end and g == 0:
                                after = {1: lambda: x_tokens(1)} if h else {3: lambda: x_tokens(0)}
                            if end and (g, h) == (1, 0):
                                before = {0: lambda: pe.wait_ge(x_tok_out, 2 * NB)}
                            unit(u0 + 4 + 2 * g + h, t0 + 8 + 4 * g, h, (act_hi, act_lo),
                                 lambda k: pe.wait_ge(act_lo_done, it * HID + (h0 + k + 1)), it, MLP_UNITS, MLP_TILES,
                                 before=before, after=after)

                quarter(0, True)
                with pe.Fori(1, QUARTERS - 1) as it:
                    quarter(it, False)
                quarter(QUARTERS - 1, False, end=layer == DEPTH - 1)
                if layer == 0:
                    post_norm(NORM["mlp_post0"], banks[t0 % 8][:])

            pe.wait_ge(const_in, 32)
            nc.tensor.transpose(banks[7][:, 0:DEPTH * 4 * KT], g_rows, ident[0:DEPTH * 4 * KT, 0:DEPTH * 4 * KT]).then_inc(gains_t, 1)
            pe.wait_ge(x_in, 16 * NB)
            pe.wait_ge(gains_out, 1)
            for k in range(KT):
                if k >= 4:
                    pe.wait_ge(x_ready, k - 3)
                for j in range(NB):
                    ins = nc.tensor.transpose(banks[x_bank(k)][:, j * P:(j + 1) * P], x_rows[:, j, k * P:(k + 1) * P], ident)
                ins.then_inc(x_t, 1)
            pe.wait_ge(setup_g, 5)

            for layer in range(DEPTH):
                name = f"in{layer}"
                u0, t0, g0 = AT[name]
                n = 2 * layer

                def swap_k(m):
                    pe.wait_ge(k_raw, 2 * layer + m - 7)
                    nc.tensor.matmul(banks[(t0 + m) % 8][:], swap_t, raw[:, m % 4, :], start=True, stop=True).then_inc(k_swapped, 1)

                fed = lambda k: pe.wait_ge(in_lo_done, n * KT + k + 1)
                if layer:
                    uq, tq, _ = AT["qi"]
                    uk, tk, _ = AT["ki"]
                    unit(uq, tq, 0, (in_hi, in_lo), fed, fresh=True)
                    unit(uq + 1, tq, 1, (in_hi, in_lo), fed, fresh=True, after=norm_steps(NORM["qi"])[0])
                    pe.wait_ge(w_lo_done, uk + 1)
                    pe.wait_ge(tile_out, tk - 7)
                    hi = w_hi[:, uk % 2, 0:KT * IDX_COLS].rearrange("p (k n) -> p k n", k=KT)
                    lo = w_lo[:, uk % 2, 0:KT * IDX_COLS].rearrange("p (k n) -> p k n", k=KT)
                    for k in range(KT):
                        if k == 4:
                            spread(NORM["qi"])
                        ins = three(banks[tk % 8][0:IDX_COLS, :], hi[:, k, :], lo[:, k, :], in_hi[:, k, :], in_lo[:, k, :], k == 0, k == KT - 1)
                    ins.then_inc(tile_done, 1)
                for g in range(A_IN_GROUPS):
                    rb_read = {m: lambda: pe.wait_ge(rb_out, n + 1)
                               for m in ((1,) if layer and g == 0 else (2,) if not layer and g == 1 else ())}
                    spread_in0 = norm_steps(NORM["in0"])[1] if not layer and g == 1 else {}
                    unit(u0 + 2 * g, t0 + 4 * g, 0, (in_hi, in_lo), fed, fresh=not layer and g == 0, before=rb_read, after=spread_in0)
                    after = {}
                    if g == 0 and layer == 0:
                        after = norm_steps(NORM["in0"])[0]
                    elif g == 2:
                        after = {2: lambda: swap_k(8), 3: lambda: swap_k(9)}
                    unit(u0 + 2 * g + 1, t0 + 4 * g, 1, (in_hi, in_lo), fed, fresh=not layer and g == 0, after=after)
                    if g == 0 and layer:
                        R = ROPE_AT["ki"]
                        pe.wait_ge(rope_done, R + 1)
                        for j in range(NB):
                            ins = nc.tensor.transpose(banks[tk % 8][:, j * IDX_COLS:(j + 1) * IDX_COLS],
                                                      roped[0:IDX_COLS, 0, j * P:(j + 1) * P], ident[0:IDX_COLS, 0:IDX_COLS])
                        ins.then_inc(wi_t, 1)
                        pe.wait_ge(ki_dup, 32)
                        pe.wait_ge(rope_lo, ROPE_AT["in1"])
                        pe.wait_ge(wi_out, 1)
                        for X in range(8 * (NB - 1)):
                            b, hd = X // 8 + 1, X % 8
                            rows = slice(64 * (hd % 2), 64 * (hd % 2) + 64)
                            if X < 4:
                                pe.wait_ge(tile_out, AT["qi"][1] + 5)
                            else:
                                pe.wait_ge(idx_relu, X - 3)
                            W, qs = (b + 1) * P, slice(b * P, (b + 1) * P)
                            three(banks[idx_bank(X)][:, 0:W], act_hi[rows, hd // 2, qs], act_lo[rows, hd // 2, qs],
                                  ki_hi[rows, 0:W], ki_lo[rows, 0:W], True, True).then_inc(idx_ready, 1)
                        pe.wait_ge(idx_relu, 8 * (NB - 1))
                for m in range(2):
                    R = ROPE_AT[name] + 10 + m
                    pe.wait_ge(v_scaled, V_AT[name] + m + 1)
                    for j in range(NB):
                        ins = nc.tensor.transpose(banks[(t0 + 10 + m) % 8][:, j * P:(j + 1) * P], roped[:, 2 + m, j * P:(j + 1) * P], ident)
                    ins.then_inc(vt_done, 1)
                attention(layer)
                u0, t0, g0 = AT[f"out{layer}"]
                pe.wait_ge(o_lo_done, 8 * (layer + 1))
                for g in range(OUT_GROUPS):
                    for h in range(2):
                        unit(u0 + 2 * g + h, t0 + 4 * g, h, (in_hi, in_lo), lambda k: None)
                post_norm(NORM[f"post{layer}"], banks[t0 % 8][:])
                mlp(layer)

            end_t = AT["end"][1]

            def y_tokens(k, js):
                pe.wait_ge(y_gained, k + 1)
                for j in js:
                    ins = nc.tensor.transpose(banks[(end_t + (k // 4) * 4 + j) % 8][:, (k % 4) * P:(k % 4 + 1) * P],
                                              y_gain[:, k, j * P:(j + 1) * P], ident)
                    if k % 4 == 3:
                        ins.then_inc(out_t, 1)

            pe.wait_ge(tile_out, end_t - 4)
            for k in range(4):
                y_tokens(k, range(NB))
            pe.wait_ge(tile_out, end_t - 1)
            for k in range(4, 7):
                y_tokens(k, range(NB - 1))
            pe.wait_ge(tile_out, end_t)
            ssq(NORM["mlp_post1"])
            y_tokens(7, range(NB - 1))
            pe.wait_ge(ms_done, NORM["mlp_post1"] + 1)
            for k in range(4, 8):
                y_tokens(k, [NB - 1])


def constants():
    import numpy as np

    c = np.zeros((P, 2 * P + 2), np.float32)
    c[:, 0:P] = np.eye(P, dtype=np.float32)
    half = ROT_DIM // 2
    inv = np.float32(500000.0) ** (-np.arange(0, ROT_DIM, 2, dtype=np.float32) / np.float32(ROT_DIM))
    for head in (0, HD):
        for f in range(half):
            c[head + f, P + head + half + f] = c[head + half + f, P + head + f] = 1.0
            c[head + f, 2 * P], c[head + half + f, 2 * P] = -1.0, 1.0
            c[head + f, 2 * P + 1] = c[head + half + f, 2 * P + 1] = inv[f]
    return c


def kernel(x, positions, norm_gains, w_mlp_up, w_mlp_down, a_w_in, a_w_out, a_sinks, b_w_in, b_w_out):
    import numpy as np
    import concourse.bacc as bacc
    from concourse.bass_utils import run_bass_kernel_spmd

    nc = bacc.Bacc("TRN2", target_bir_lowering=False, num_devices=1, dynamic_dma_scratch_size=1024)
    arrays, args = {}, []
    for name, a, shape in (
        ("x", x, (SEQ, D)), ("positions", positions, (1, SEQ)), ("norm_gains", norm_gains, (DEPTH * 4 * KT, P)),
        ("w_mlp_up", w_mlp_up, (DEPTH, D, FF)), ("w_mlp_down", w_mlp_down, (DEPTH, FF, D)),
        ("a_w_in", a_w_in, (D, QD + 2 * KVD)), ("a_w_out", a_w_out, (QD, D)), ("a_sinks", a_sinks, (1, NH)),
        ("b_w_in", b_w_in, (D, QD + 2 * KVD + IDX_HEADS * IDX_DIM + IDX_DIM + IDX_HEADS)), ("b_w_out", b_w_out, (QD, D)),
        ("consts", constants(), (P, 2 * P + 2)),
    ):
        a = np.ascontiguousarray(a).reshape(shape)
        arrays[f"in_{name}"] = a
        args.append(nc.dram_tensor(f"in_{name}", a.shape, mybir.dt.from_np(a.dtype), kind="ExternalInput").ap())
    out = nc.dram_tensor("out", (SEQ, D), mybir.dt.float32, kind="ExternalOutput").ap()
    hybrid_trunk(nc, *args, out)
    r = run_bass_kernel_spmd(nc, [arrays], core_ids=[0])
    return r.results[0]["out"].reshape(1, SEQ, D)
```
